# Optimizing a Trainium2 kernel written in Bass

```python
import jax, jax.numpy as jnp
from jax import lax
import numpy as np

D_MODEL = 1024
BATCH = 1
SEQ = 512
DEPTH = 1

HEAD_DIM = 64
A_GROUPS = ((128, 1), (512, 4), (2048, 16))
A_HEADS = 4
B_Q_HEADS = 8
B_KV_HEADS = 2
B_GROUP = B_Q_HEADS // B_KV_HEADS
B_WINDOW = 128
C_HEADS = 4
X_HEADS = 4
MEM_LEN = 256
D_FF = -(-8 * D_MODEL // (3 * 256)) * 256
NUM_BUCKETS = 32
MAX_DISTANCE = 2048
BLOCK = 128
N_A_BIAS = len(A_GROUPS) * A_HEADS
N_BIAS_HEADS = N_A_BIAS + B_Q_HEADS
FGATE_BIAS = 3.0
NEG_INF = -1e30
LN_EPS = 1e-5
ALPHA = (2 * DEPTH) ** 0.25
BETA = (8 * DEPTH) ** -0.25

IN_SPLITS = (
    len(A_GROUPS) * A_HEADS * HEAD_DIM,
    len(A_GROUPS) * A_HEADS * HEAD_DIM,
    len(A_GROUPS) * A_HEADS * HEAD_DIM,
    B_Q_HEADS * HEAD_DIM,
    B_KV_HEADS * HEAD_DIM,
    B_KV_HEADS * HEAD_DIM,
    C_HEADS * HEAD_DIM,
    C_HEADS * HEAD_DIM,
    C_HEADS * HEAD_DIM,
    C_HEADS,
    3 * D_MODEL,
)
IN_WIDTH = sum(IN_SPLITS)
SPLIT_POINTS = [int(p) for p in np.cumsum(IN_SPLITS)[:-1]]

kernel_name = "hybrid_dilated_swa_fox_deepnorm"

def layer_norm(x, g, b):
    xf = x.astype(jnp.float32)
    mu = jnp.mean(xf, axis=-1, keepdims=True)
    var = jnp.mean(jnp.square(xf - mu), axis=-1, keepdims=True)
    return ((xf - mu) * lax.rsqrt(var + LN_EPS) * g + b).astype(x.dtype)

def t5_bucket(dist):
    max_exact = NUM_BUCKETS // 2
    safe = np.maximum(dist, max_exact).astype(np.float32)
    large = max_exact + (np.log(safe / max_exact) / np.log(MAX_DISTANCE / max_exact)
                         * (NUM_BUCKETS - max_exact)).astype(np.int32)
    large = np.minimum(large, NUM_BUCKETS - 1)
    return np.where(dist < max_exact, dist, large).astype(np.int32)

def band_geometry(n_blocks, window, dilation):
    i = np.arange(BLOCK)[:, None]
    j = np.arange(2 * BLOCK)[None, :]
    delta = i + BLOCK - j
    band = (delta >= 0) & (delta <= window)
    k_abs = np.arange(n_blocks)[:, None, None] * BLOCK + j[None] - BLOCK
    mask = band[None] & (k_abs >= 0)
    buckets = t5_bucket(np.maximum(delta, 0) * dilation)
    return mask, buckets

def banded_attention(q, k, v, bias, mask, sinks=None):
    N, L, Hkv, G, dh = q.shape
    nb = mask.shape[0]
    pad = nb * BLOCK - L
    q = jnp.pad(q, ((0, 0), (0, pad), (0, 0), (0, 0), (0, 0)))
    k = jnp.pad(k, ((0, 0), (BLOCK, pad), (0, 0), (0, 0)))
    v = jnp.pad(v, ((0, 0), (BLOCK, pad), (0, 0), (0, 0)))
    qb = q.reshape(N, nb, BLOCK, Hkv, G, dh)
    kb = k.reshape(N, nb + 1, BLOCK, Hkv, dh)
    vb = v.reshape(N, nb + 1, BLOCK, Hkv, dh)
    kw = jnp.concatenate([kb[:, :-1], kb[:, 1:]], axis=2)
    vw = jnp.concatenate([vb[:, :-1], vb[:, 1:]], axis=2)
    s = jnp.einsum('nbqhgd,nbkhd->nbhgqk', qb, kw).astype(jnp.float32) + bias
    s = jnp.where(mask[None, :, None, None], s, NEG_INF)
    m = jnp.max(s, axis=-1, keepdims=True)
    if sinks is not None:
        sink = sinks.astype(jnp.float32)[None, None, :, :, None, None]
        m = jnp.maximum(m, sink)
    p = jnp.exp(s - m)
    denom = jnp.sum(p, axis=-1, keepdims=True)
    if sinks is not None:
        denom = denom + jnp.exp(sink - m)
    o = jnp.einsum('nbhgqk,nbkhd->nbqhgd', (p / denom).astype(v.dtype), vw)
    lse = (m + jnp.log(denom))[..., 0]
    o = o.reshape(N, nb * BLOCK, Hkv, G, dh)[:, :L]
    lse = lse.transpose(0, 1, 4, 2, 3).reshape(N, nb * BLOCK, Hkv, G)[:, :L]
    return o, lse

def dilated_attention(qa, ka, va, rel_bias):
    Bsz, S = qa.shape[:2]
    outs, lses = [], []
    for g, (window, dil) in enumerate(A_GROUPS):
        L = S // dil
        nb = -(-L // BLOCK)
        mask, buckets = band_geometry(nb, window // dil, dil)
        bias = rel_bias[buckets][..., g * A_HEADS:(g + 1) * A_HEADS].astype(jnp.float32)
        bias = bias.transpose(2, 0, 1)[:, None]

        def strided(t):
            return t.reshape(Bsz, L, dil, A_HEADS, HEAD_DIM).transpose(0, 2, 1, 3, 4).reshape(
                Bsz * dil, L, A_HEADS, HEAD_DIM)

        o, lse = banded_attention(strided(qa[:, :, g])[:, :, :, None], strided(ka[:, :, g]),
                                  strided(va[:, :, g]), bias, mask)
        o = o[:, :, :, 0].reshape(Bsz, dil, L, A_HEADS, HEAD_DIM).transpose(0, 2, 1, 3, 4)
        lse = lse[..., 0].reshape(Bsz, dil, L, A_HEADS).transpose(0, 2, 1, 3)
        outs.append(o.reshape(Bsz, S, A_HEADS, HEAD_DIM))
        lses.append(lse.reshape(Bsz, S, A_HEADS))
    o = jnp.stack(outs, axis=0)
    wts = jax.nn.softmax(jnp.stack(lses, axis=0), axis=0)
    o = jnp.einsum('gbsh,gbshd->bshd', wts.astype(o.dtype), o)
    return o.reshape(Bsz, S, A_HEADS * HEAD_DIM)

def window_gqa_with_sinks(qb, kb, vb, sinks, rel_bias):
    Bsz, S = qb.shape[:2]
    mask, buckets = band_geometry(S // BLOCK, B_WINDOW - 1, 1)
    bias = rel_bias[buckets][..., N_A_BIAS:N_BIAS_HEADS].astype(jnp.float32)
    bias = bias.transpose(2, 0, 1).reshape(B_KV_HEADS, B_GROUP, BLOCK, 2 * BLOCK)
    o, _ = banded_attention(qb, kb, vb, bias, mask, sinks)
    return o.reshape(Bsz, S, B_Q_HEADS * HEAD_DIM)

def forgetting_attention(qc, kc, vc, fgate_logit):
    Bsz, S, H, dh = qc.shape
    nb = S // BLOCK
    c = jnp.cumsum(jax.nn.log_sigmoid(fgate_logit.astype(jnp.float32)), axis=1)
    qblk = qc.reshape(Bsz, nb, BLOCK, H, dh).transpose(1, 0, 2, 3, 4)
    cblk = c.reshape(Bsz, nb, BLOCK, H).transpose(1, 0, 2, 3)
    c_k = c.transpose(0, 2, 1)
    kpos = jnp.arange(S)

    def one_block(args):
        q_i, c_i, blk = args
        s = jnp.einsum('bqhd,bkhd->bhqk', q_i, kc).astype(jnp.float32)
        s = s + c_i.transpose(0, 2, 1)[..., None] - c_k[:, :, None, :]
        qpos = blk * BLOCK + jnp.arange(BLOCK)
        s = jnp.where(kpos[None, :] <= qpos[:, None], s, NEG_INF)
        p = jax.nn.softmax(s, axis=-1)
        return jnp.einsum('bhqk,bkhd->bqhd', p.astype(vc.dtype), vc)

    o = lax.map(one_block, (qblk, cblk, jnp.arange(nb)))
    return o.transpose(1, 0, 2, 3, 4).reshape(Bsz, S, H * dh)

def hybrid_mixer(x, w_in, b_in, sinks, w_a, w_b, w_c, w_out, rel_bias):
    Bsz, S, _ = x.shape
    proj = x @ w_in + b_in
    qa, ka, va, qb, kb, vb, qc, kc, vc, fc, gates = jnp.split(proj, SPLIT_POINTS, axis=-1)
    scale = HEAD_DIM ** -0.5
    na = len(A_GROUPS)
    o_a = dilated_attention((qa * scale).reshape(Bsz, S, na, A_HEADS, HEAD_DIM),
                            ka.reshape(Bsz, S, na, A_HEADS, HEAD_DIM),
                            va.reshape(Bsz, S, na, A_HEADS, HEAD_DIM), rel_bias)
    o_b = window_gqa_with_sinks((qb * scale).reshape(Bsz, S, B_KV_HEADS, B_GROUP, HEAD_DIM),
                                kb.reshape(Bsz, S, B_KV_HEADS, HEAD_DIM),
                                vb.reshape(Bsz, S, B_KV_HEADS, HEAD_DIM),
                                sinks.reshape(B_KV_HEADS, B_GROUP), rel_bias)
    o_c = forgetting_attention((qc * scale).reshape(Bsz, S, C_HEADS, HEAD_DIM),
                               kc.reshape(Bsz, S, C_HEADS, HEAD_DIM),
                               vc.reshape(Bsz, S, C_HEADS, HEAD_DIM), fc)
    g = jax.nn.sigmoid(gates.astype(jnp.float32)).astype(x.dtype).reshape(Bsz, S, 3, D_MODEL)
    merged = g[:, :, 0] * (o_a @ w_a) + g[:, :, 1] * (o_b @ w_b) + g[:, :, 2] * (o_c @ w_c)
    return merged @ w_out

def memory_cross_attention(x, mem, w_q, w_kv, w_o):
    Bsz, S, _ = x.shape
    M = mem.shape[1]
    q = (x @ w_q).reshape(Bsz, S, X_HEADS, HEAD_DIM) * (HEAD_DIM ** -0.5)
    k, v = jnp.split(mem @ w_kv, 2, axis=-1)
    k = k.reshape(Bsz, M, X_HEADS, HEAD_DIM)
    v = v.reshape(Bsz, M, X_HEADS, HEAD_DIM)
    p = jax.nn.softmax(jnp.einsum('bshd,bmhd->bhsm', q, k).astype(jnp.float32), axis=-1)
    o = jnp.einsum('bhsm,bmhd->bshd', p.astype(v.dtype), v).reshape(Bsz, S, X_HEADS * HEAD_DIM)
    return o @ w_o

def swiglu(x, w_in, w_out):
    a, b = jnp.split(x @ w_in, 2, axis=-1)
    return (jax.nn.silu(a) * b) @ w_out

def setup_inputs(seed: int = 0) -> dict:
    key = jax.random.key(seed)
    ks = jax.random.split(key, 24)

    def nrm(k, shape, scale):
        return jax.random.normal(k, shape, jnp.float32) * scale

    offs = np.concatenate([[0], np.cumsum(IN_SPLITS)])
    col_scale = np.ones((IN_WIDTH,), np.float32)
    for idx in (2, 5, 8):
        col_scale[offs[idx]:offs[idx + 1]] = BETA
    bias_shift = np.zeros((IN_WIDTH,), np.float32)
    bias_shift[offs[9]:offs[10]] = FGATE_BIAS
    xkv_scale = np.concatenate([np.ones((X_HEADS * HEAD_DIM,), np.float32),
                                np.full((X_HEADS * HEAD_DIM,), BETA, np.float32)])
    wa_in = A_HEADS * HEAD_DIM
    wb_in = B_Q_HEADS * HEAD_DIM
    wc_in = C_HEADS * HEAD_DIM
    wx = X_HEADS * HEAD_DIM
    return {
        "x": nrm(ks[0], (BATCH, SEQ, D_MODEL), 1.0),
        "mem": nrm(ks[1], (BATCH, MEM_LEN, D_MODEL), 1.0),
        "w_in": nrm(ks[2], (DEPTH, D_MODEL, IN_WIDTH), D_MODEL ** -0.5) * jnp.asarray(col_scale),
        "b_in": nrm(ks[3], (DEPTH, IN_WIDTH), 0.02) + jnp.asarray(bias_shift),
        "attn_sinks": nrm(ks[4], (DEPTH, B_Q_HEADS), 0.5),
        "w_branch_a": nrm(ks[5], (DEPTH, wa_in, D_MODEL), wa_in ** -0.5 * BETA),
        "w_branch_b": nrm(ks[6], (DEPTH, wb_in, D_MODEL), wb_in ** -0.5 * BETA),
        "w_branch_c": nrm(ks[7], (DEPTH, wc_in, D_MODEL), wc_in ** -0.5 * BETA),
        "w_mix_out": nrm(ks[8], (DEPTH, D_MODEL, D_MODEL), D_MODEL ** -0.5 * BETA),
        "ln1_g": 1.0 + nrm(ks[9], (DEPTH, D_MODEL), 0.02),
        "ln1_b": nrm(ks[10], (DEPTH, D_MODEL), 0.02),
        "w_xq": nrm(ks[11], (DEPTH, D_MODEL, wx), D_MODEL ** -0.5),
        "w_xkv": nrm(ks[12], (DEPTH, D_MODEL, 2 * wx), D_MODEL ** -0.5) * jnp.asarray(xkv_scale),
        "w_xo": nrm(ks[13], (DEPTH, wx, D_MODEL), wx ** -0.5 * BETA),
        "ln2_g": 1.0 + nrm(ks[14], (DEPTH, D_MODEL), 0.02),
        "ln2_b": nrm(ks[15], (DEPTH, D_MODEL), 0.02),
        "w_ffn_in": nrm(ks[16], (DEPTH, D_MODEL, 2 * D_FF), D_MODEL ** -0.5 * BETA),
        "w_ffn_out": nrm(ks[17], (DEPTH, D_FF, D_MODEL), D_FF ** -0.5 * BETA),
        "ln3_g": 1.0 + nrm(ks[18], (DEPTH, D_MODEL), 0.02),
        "ln3_b": nrm(ks[19], (DEPTH, D_MODEL), 0.02),
        "rel_bias": nrm(ks[20], (NUM_BUCKETS, N_BIAS_HEADS), 0.5),
    }

def reference(x, mem, w_in, b_in, attn_sinks, w_branch_a, w_branch_b, w_branch_c, w_mix_out,
              ln1_g, ln1_b, w_xq, w_xkv, w_xo, ln2_g, ln2_b, w_ffn_in, w_ffn_out,
              ln3_g, ln3_b, rel_bias):
    for l in range(DEPTH):
        h = hybrid_mixer(x, w_in[l], b_in[l], attn_sinks[l], w_branch_a[l], w_branch_b[l],
                         w_branch_c[l], w_mix_out[l], rel_bias)
        x = layer_norm(ALPHA * x + h, ln1_g[l], ln1_b[l])
        h = memory_cross_attention(x, mem, w_xq[l], w_xkv[l], w_xo[l])
        x = layer_norm(ALPHA * x + h, ln2_g[l], ln2_b[l])
        h = swiglu(x, w_ffn_in[l], w_ffn_out[l])
        x = layer_norm(ALPHA * x + h, ln3_g[l], ln3_b[l])
    return x


_drawn_inputs = setup_inputs


def setup_inputs(seed=0):
    import zlib

    import numpy as np

    out = dict(_drawn_inputs(seed))
    spreads = {}
    factors = {'attn_sinks': 30.181,
     'w_branch_a': 3.544,
     'w_branch_b': 3.098,
     'ln1_g': 7.702,
     'ln1_b': 7.868,
     'ln2_g': 7.864,
     'ln2_b': 7.782,
     'ln3_g': 8.474,
     'ln3_b': 8.274,
     'rel_bias': 6.383}
    for name, (base, spread) in spreads.items():
        noise = np.random.default_rng([zlib.crc32(name.encode()), seed]).standard_normal(out[name].shape)
        drawn = base * np.exp(spread * noise) if base else spread * noise
        out[name] = __import__('jax').numpy.asarray(drawn.astype(out[name].dtype))
    for name, factor in factors.items():
        out[name] = (out[name] * factor).astype(out[name].dtype)
    return out
```

```python
from contextlib import ExitStack

import numpy as np
import concourse.bass as bass
from concourse import mybir
from concourse.alu_op_type import AluOpType as ALU

F32 = mybir.dt.float32
F32R = mybir.dt.float32r
BF16 = mybir.dt.bfloat16
ACT = mybir.ActivationFunctionType

P = 128
D = 1024
SEQ = 512
MEM = 256
DH = 64
KT = D // P
TT = SEQ // P
N_AH, N_G = 4, 3
N_BH, N_BKV, N_CH, N_XH = 8, 2, 4, 4
D_FF = 2816
N_BIAS = N_G * N_AH + N_BH
N_BUCKETS, MAX_DIST = 32, 2048
ALPHA = 2.0 ** 0.25
LN_EPS = 1e-5
SCALE = DH ** -0.5
MASK = -1e30
HUGE = 3e38

QA, KA, VA0 = 0, 768, 1536
QB, KB, VB0 = 2304, 2816, 2944
QC, KC, VC0 = 3072, 3328, 3584
FC = 3840
GATES = 3844
IN_W = GATES + 3 * D
VBC_N = 128 + 256 + 4

SEG1, SEG4, SEG16 = 3 * P - 1, 2 * P - 1, 2 * P - 1
SEG_N = SEG1 + SEG4 + SEG16
PT_SLOTS = 3
SEG_CUT = 448


def t5_bucket(dist):
    exact = N_BUCKETS // 2
    safe = np.maximum(dist, exact).astype(np.float32)
    large = exact + (np.log(safe / exact) / np.log(MAX_DIST / exact) * (N_BUCKETS - exact)).astype(np.int32)
    return np.where(dist < exact, dist, np.minimum(large, N_BUCKETS - 1)).astype(np.int32)


def table_constants():
    d1 = 2 * P - 1 - np.arange(SEG1)
    d4 = P - 1 - np.arange(SEG4)
    dist = np.concatenate([d1, 4 * d4, 4 * d4])
    bucket = t5_bucket(np.maximum(dist, 0))
    one_hot = (np.arange(N_BUCKETS)[:, None] == bucket[None]).astype(np.float32)
    a1 = np.where((d1 >= 0) & (d1 <= 128), 0.0, MASK)
    b1 = np.where((d1 >= 0) & (d1 <= 127), 0.0, MASK)
    a4 = np.where(d4 >= 0, 0.0, MASK)
    a16 = np.where((d4 >= 0) & (d4 % 4 == 0), 0.0, MASK)
    heads = [np.concatenate([b1 if h >= N_G * N_AH else a1, a4, a16]) for h in range(N_BIAS)]
    return one_hot, np.stack(heads).astype(np.float32)


T_QA, T_KA, T_QB, T_KB, T_QC, T_KC, T_N = 0, 6, 12, 16, 18, 20, 22
OUT_TILES = [0, 1, 12, 13, 14, 15, 18, 19]

PV0 = 0
PV12 = 2
PQA = 6
PVBC = 18
PQB = 22
PG = 31
PM = 63
PKX = 71
PVX = 73
PXQ = 75
PXO = 77
PF = 79
PO = PF + 2 * (D_FF // P)
P_END = PO + D_FF // P
N_PAIR = D // 256
FF_T = D_FF // P
FF_PAIR = FF_T // 2

FRONT = ([("scores", 0), ("piece", 18), ("piece", 19), ("piece", 20), ("scores", 1), ("piece", 21), ("piece", 22),
          ("scores", 2), ("piece", 23), ("piece", 24), ("piece", 25), ("scores", 3), ("piece", 26), ("piece", 27),
          ("forward", 0), ("piece", 28), ("piece", 29), ("back", 0), ("piece", 30)])
BACKHALF = [x for j in range(8) for x in (("output", j), ("scores", j + 4))] + [("output", j) for j in range(8, 12)]
MIX_ORDER = [2, 3, 0, 1]


def band_at(t):
    return 0 if t == 0 else P + (t - 1) * 256


C_AT = [0, 128, 384, 768]


def band_groups(base):
    own = [base + band_at(t) + (P if t else 0) for t in range(TT)]
    prev = [None] + [base + band_at(t) for t in range(1, TT)]
    return [([own[0], prev[1], own[1], prev[2]], [(0, 0, 256, 0), (1, 256, 256, 128)]),
            ([own[2], prev[3], own[3]], [(2, 0, 256, 256), (3, 256, 128, 384)])]


def make_jobs():
    jobs = []
    for h in range(N_AH):
        banks = [[("A0", h, 0, 0, 128, 0), ("A0", h, 1, 128, 256, 128)],
                 [("A0", h, 2, 0, 256, 384), ("A0", h, 3, 256, 256, 640)],
                 [("A1", h, s, s * P, P, 896 + s * P) for s in range(TT)],
                 [("A2", h, s, s * P, P, 1408 + s * P) for s in range(TT)]]
        g0 = band_groups(0)
        groups = [(g0[0][0], g0[0][1], "A0", h, True, False), (g0[1][0], g0[1][1], "A0", h, False, True)]
        for kind, base, first in (("A1", 896, True), ("A2", 1408, False)):
            groups.append(([base + s * P for s in range(TT)], [(s, s * P, P, s * P) for s in range(TT)],
                           kind, h, first, not first))
        jobs.append((banks, groups))
    for pair in range(N_BH // 2):
        banks, groups = [], []
        for i in range(2):
            h, base = 2 * pair + i, 1024 * i
            banks += [[("B", h, 0, 0, 128, base), ("B", h, 1, 128, 256, base + 128)],
                      [("B", h, 2, 0, 256, base + 384), ("B", h, 3, 256, 256, base + 640)]]
            g = band_groups(base)
            groups += [(g[0][0], g[0][1], "B", h, True, False), (g[1][0], g[1][1], "B", h, False, True)]
        jobs.append((banks, groups))
    for h in range(N_CH):
        banks = [[("C", h, 0, 0, 128, C_AT[0]), ("C", h, 2, 128, 384, C_AT[2])],
                 [("C", h, 1, 0, 256, C_AT[1])], [("C", h, 3, 0, 512, C_AT[3])]]
        groups = [([C_AT[t] for t in range(4)], [(0, 0, 512, 0)], "C", h, True, False),
                  ([C_AT[1] + P, C_AT[2] + P, C_AT[3] + P, C_AT[3] + 3 * P],
                   [(1, 0, 384, 128), (3, 384, 128, 384)], "C", h, False, False),
                  ([C_AT[2] + 2 * P, C_AT[3] + 2 * P], [(2, 0, 256, 256)], "C", h, False, True)]
        jobs.append((banks, groups))
    return jobs


def make_cross_jobs():
    jobs = []
    for h in range(N_XH):
        banks = [[("X", h, 2 * b + i, 256 * i, 256, 256 * (2 * b + i)) for i in range(2)] for b in range(2)]
        groups = [([256 * t + P * m for t in range(TT)], [(m, 0, 512, 0)], "X", h, m == 0, m == 1) for m in range(2)]
        jobs.append((banks, groups))
    return jobs


def build_layer(nc, A, out):
    JOBS = make_jobs() + make_cross_jobs()
    N_SELF = 12
    N_JOB = len(JOBS)
    units_before, groups_before = [0], [0]
    for banks, groups in JOBS:
        units_before.append(units_before[-1] + sum(map(len, banks)))
        groups_before.append(groups_before[-1] + len(groups))
    bank_list = [(j, b) for j, (banks, _) in enumerate(JOBS) for b in range(len(banks))]
    bank_index = {jb: n for n, jb in enumerate(bank_list)}
    bank_units_end = {}
    n = 0
    for j, b in bank_list:
        n += len(JOBS[j][0][b])
        bank_units_end[(j, b)] = n
    group_list = [(j, g) for j, (_, groups) in enumerate(JOBS) for g in range(len(groups))]
    group_index = {jg: n for n, jg in enumerate(group_list)}
    acc_end, acc_of, acc_kind = [], {}, []
    for n, (j, g) in enumerate(group_list):
        grp = JOBS[j][1][g]
        if grp[4]:
            acc_end.append(None)
            acc_kind.append((grp[2], grp[3]))
        acc_of[n] = len(acc_end) - 1
        if grp[5]:
            acc_end[-1] = n
    N_ACC = len(acc_end)
    acc_by_dve = [k == "A1" for k, _ in acc_kind]
    acc_count = []
    c_act = c_dve = 0
    for by_dve in acc_by_dve:
        c_dve += by_dve
        c_act += not by_dve
        acc_count.append(c_dve if by_dve else c_act)
    accs_after = {j: [m for m in range(N_ACC) if group_list[acc_end[m]][0] == j] for j in range(N_JOB)}
    SLOT = lambda j: j % 4

    w_in = A["w_in"][0].rearrange("(k p) n -> p k n", p=P)
    w_mix = A["w_mix_out"][0].rearrange("(k p) n -> p k n", p=P)
    w_br = [A[f"w_branch_{x}"][0].rearrange("(k p) n -> p k n", p=P) for x in "abc"]
    w_xkv = A["w_xkv"][0].rearrange("(k p) n -> p k n", p=P)
    w_xq = A["w_xq"][0].rearrange("(k p) n -> p k n", p=P)
    w_xo = A["w_xo"][0].rearrange("(k p) n -> p k n", p=P)
    w_f1 = A["w_ffn_in"][0].rearrange("(k p) n -> p k n", p=P)
    w_f2 = A["w_ffn_out"][0].rearrange("(k p) n -> p k n", p=P)
    rows1 = nc.dram_tensor("rows1", (N_AH + N_BH, P, SEG1), F32, kind="Internal")
    rows4 = nc.dram_tensor("rows4", (N_AH, P, SEG4), F32, kind="Internal")
    rows16 = nc.dram_tensor("rows16", (N_AH, P, SEG16), F32, kind="Internal")

    with ExitStack() as ctx:
        def sem(name):
            return ctx.enter_context(nc.semaphore(name))

        def sb(name, shape, dt=F32, stack=None):
            return (stack or ctx).enter_context(nc.sbuf_tensor(name, shape, dt))

        raw = [sb(f"raw{i}", [P, 2048]) for i in range(2)]
        w_hi = [sb(f"w_hi{i}", [P, 1024], F32R) for i in range(2)]
        w_lo = [sb(f"w_lo{i}", [P, 1024], F32R) for i in range(2)]
        xt_hi = sb("xt_hi", [P, KT, SEQ], F32R)
        xt_lo = sb("xt_lo", [P, KT, SEQ], F32R)
        ident = sb("ident", [P, P])
        shift = sb("shift", [P, 896], BF16)
        spread = sb("spread", [P, 516], BF16)
        upper = sb("upper", [P, 256], BF16)
        causal = sb("causal", [P, P])
        bias_t = sb("bias_t", [P, 54])
        sink = sb("sink", [P, N_BH])
        neg_sink = sb("neg_sink", [P, N_BH])
        stat_a = sb("stat_a", [P, TT, N_G, 2, N_AH])
        stat_nat = sb("stat_nat", [P, TT, N_G, 2, N_AH])
        parts = sb("parts", [P, 3, TT * N_G * 2 * N_AH], BF16)
        rest = sb("rest", [P, TT * N_G * 2 * N_AH])
        moved = sb("moved", [P, TT * 2 * 24])
        comb_min = sb("comb_min", [P, TT, N_AH])
        comb_e = sb("comb_e", [P, TT, N_G, N_AH])
        comb_z = sb("comb_z", [P, TT, N_G, N_AH])
        factor = sb("factor", [P, TT, N_G, N_AH])
        factor_s = sb("factor_s", [P, 2, TT, N_AH])
        nmax = sb("nmax", [P, 64])
        psum_ = sb("psum_", [P, 64])
        rsum = sb("rsum", [P, 64])
        esink = sb("esink", [P, N_BH * TT])
        fl = sb("fl", [P, 3, TT, N_CH])
        logf = sb("logf", [P, TT, N_CH])
        lparts = sb("lparts", [P, 3, TT * N_CH], BF16)
        cum = sb("cum", [P, TT, N_CH])
        cum3 = sb("cum3", [P, TT, 3, N_CH])
        ncum_t = sb("ncum_t", [N_CH, SEQ])
        bn = sb("bn", [P, TT, 2, 6])
        mv = sb("mv", [P, TT, 2])
        rstd = sb("rstd", [P, TT, 3])
        half = sb("half", [P, 1])

        with ExitStack() as st:
            memt_hi = sb("memt_hi", [P, KT, MEM], F32R, st)
            memt_lo = sb("memt_lo", [P, KT, MEM], F32R, st)
        sa = sb("sa", [P, 2, 512])
        ht = sb("ht", [P, 512])
        sb("hold_mem", [P, 2 * KT * MEM - 3 * 512])

        with ExitStack() as st:
            qk = sb("qk", [P, T_N, SEQ], F32, st)
            va = sb("va", [P, TT, 768], F32, st)
            vbc = sb("vbc", [P, TT, VBC_N], F32, st)
            tab1 = sb("tab1", [P, N_AH + N_BH, 256], F32, st)
            tab4 = sb("tab4", [P, N_AH, P], F32, st)
            tab16 = sb("tab16", [P, N_AH, P], F32, st)
            prob = sb("prob", [P, 4, 2048], F32, st)
            pt = sb("pt", [P, PT_SLOTS, 512], F32, st)
        with ExitStack() as st:
            sb("hold_qk", [P, T_N * SEQ + TT * 768 + TT * VBC_N], F32, st)
            mem_nat = sb("mem_nat", [P, 2, D], F32, st)
            sb("hold_tab", [P, (N_AH + N_BH) * 256 - 2 * D + 2 * N_AH * P], F32, st)
            x_nat = sb("x_nat", [P, TT, D], F32, st)
            one_hot = sb("one_hot", [N_BUCKETS, SEG_N], F32, st)
            seg_mask = sb("seg_mask", [N_BIAS, SEG_N], F32, st)
            seg_row = sb("seg_row", [N_BIAS, SEG_N], F32, st)
            b_rows = sb("b_rows", [54, P], F32, st)
            rel = sb("rel", [N_BUCKETS, N_BIAS], F32, st)
            sb("hold_p", [P, 4 * 2048 - TT * D - 3 * SEG_N - P - N_BIAS], F32, st)
            bv = sb("bv", [P, 768 + VBC_N], F32, st)
        with ExitStack() as keep:
            resid = sb("resid", [P, TT, D], F32, keep)
            gb = sb("gb", [P, 2, D], F32, keep)
            with ExitStack() as st:
                sg = sb("sg", [P, 6, 512], F32, st)
                mt = sb("mt", [P, 3, 512], F32, st)
                sb("pad", [P, 512], F32, st)
                with ExitStack() as st2:
                    o_hi = sb("o_hi", [P, KT, SEQ], F32R, st2)
                    o_lo = sb("o_lo", [P, KT, SEQ], F32R, st2)
                    m_hi = sb("m_hi", [P, KT, SEQ], F32R, st2)
                    m_lo = sb("m_lo", [P, KT, SEQ], F32R, st2)
                kx = sb("kx", [P, 2, MEM], F32, st)
                vx = sb("vx", [P, 2, N_XH * DH], F32, st)
                zero = sb("zero", [P, 256], F32, st)
                sb("hold_o", [P, 2 * KT * SEQ - 2 * MEM - 2 * N_XH * DH - 256], F32, st)
                qx = sb("qx", [P, 2, SEQ], F32, st)
                probx = sb("probx", [P, 4, 1024], F32, st)
                ptx = sb("ptx", [P, PT_SLOTS, 512], F32, st)
                ox_hi = sb("ox_hi", [P, 2, SEQ], F32R, st)
                ox_lo = sb("ox_lo", [P, 2, SEQ], F32R, st)
            with ExitStack() as st:
                h_hi = sb("h_hi", [P, FF_T, SEQ], F32R, st)
                h_lo = sb("h_lo", [P, FF_T, SEQ], F32R, st)

        ps = ctx.enter_context(nc.psum_tensor("ps", [P, 8, 512], F32))

        raw_in = [sem(f"raw_in{i}") for i in range(2)]
        hi_done, lo_done, piece_done = sem("hi_done"), sem("lo_done"), sem("piece_done")
        x_in = [sem(f"x_in{t}") for t in range(TT)]
        mem_in, small_in, resid_in = sem("mem_in"), sem("small_in"), sem("resid_in")
        const_ready = sem("const_ready")
        turned, turn_hi, turn_lo = sem("turned"), sem("turn_hi"), sem("turn_lo")
        mem_turned, mem_hi, mem_lo = sem("mem_turned"), sem("mem_hi"), sem("mem_lo")
        seg_ps, seg_ready, seg_out, table_in = sem("seg_ps"), sem("seg_ready"), sem("seg_out"), sem("table_in")
        proj_out = sem("proj_out")
        score_ps, ncum_ps, base_ready, diag_ready = sem("score_ps"), sem("ncum_ps"), sem("base_ready"), sem("diag_ready")
        neg_ready, exp_done, rsum_ready, prob_ready = sem("neg_ready"), sem("exp_done"), sem("rsum_ready"), sem("prob_ready")
        esink_done = sem("esink_done")
        pt_ps, pt_act, pt_dve, av_done = sem("pt_ps"), sem("pt_act"), sem("pt_dve"), sem("av_done")
        acc_act, acc_dve = sem("acc_act"), sem("acc_dve")
        dve_step = sem("dve_step")
        pool_step = sem("pool_step")
        parts_ready, moved_ps, moved_out, diff_ready, comb_exp = (sem("parts_ready"), sem("moved_ps"), sem("moved_out"),
                                                                 sem("diff_ready"), sem("comb_exp"))
        fparts_ready, back_ps, factor_ready = sem("fparts_ready"), sem("back_ps"), sem("factor_ready")
        abs_ready, act_f, lparts_ready, cum_ps, cum_ready, cumt_ps, cumt_out = (
            sem("abs_ready"), sem("act_f"), sem("lparts_ready"), sem("cum_ps"), sem("cum_ready"), sem("cumt_ps"), sem("cumt_out"))
        o_hi_done, o_lo_done = sem("o_hi_done"), sem("o_lo_done")
        branch_ps, sig_done, merged_even, merged_odd, m_ready = (sem("branch_ps"), sem("sig_done"), sem("merged_even"),
                                                                 sem("merged_odd"), sem("m_ready"))
        merge_step, ffn_step = sem("merge_step"), sem("ffn_step")
        rows_done, y_done, var_done, rstd_done, norm_done, gb_done, gb_in = (
            sem("rows_done"), sem("y_done"), sem("var_done"), sem("rstd_done"), sem("norm_done"), sem("gb_done"), sem("gb_in"))
        memkv_out, xq_out, zero_ready = sem("memkv_out"), sem("xq_out"), sem("zero_ready")
        oxh_done, oxl_done = sem("oxh_done"), sem("oxl_done")
        silu_done, h_done = sem("silu_done"), sem("h_done")
        stored = sem("stored")

        def stat_col(kind, h, t):
            return {"B": 0, "C": 32, "X": 48}[kind] + h * TT + t

        def score_bank(j, b):
            return b if j < N_SELF else 2 * (j % 2) + b

        def raw_piece(p):
            hi, lo = w_hi[p % 2], w_lo[p % 2]
            i, slot = piece_place(p)
            r = raw[slot]
            if p == PQB + 4:
                return r[:, 0:1024], hi[:, 0:1024], lo[:, 0:1024]
            if PVBC <= p < PQB:
                n = 2 * VBC_N
                return r[:, i * n:(i + 1) * n], hi[:, 0:n], lo[:, 0:n]
            if is_tile_piece(p):
                v = r[:, :].rearrange("p (k c) -> p k c", k=KT)[:, :, i * P:(i + 1) * P]
                return v, hi[:, :].rearrange("p (k c) -> p k c", k=KT), lo[:, :].rearrange("p (k c) -> p k c", k=KT)
            return r[:, i * 1024:(i + 1) * 1024], hi[:, :], lo[:, :]

        def is_tile_piece(p):
            return PQA <= p < PVBC or PQB <= p < PM or PKX <= p < PVX or PXQ <= p < PXO or PF <= p < PO

        def chunk_of(p):
            return p // 2 if p < PQB + 4 else (PQB + 4) // 2 if p == PQB + 4 else (p + 1) // 2

        def piece_place(p):
            c = chunk_of(p)
            first = 2 * c if p <= PQB + 4 else 2 * c - 1
            return p - first, c % 2

        def last_piece(c):
            return 2 * c + 1 if c < 13 else 2 * c if c >= 13 else None

        def chunk_loads(c):
            r = raw[c % 2]
            k8 = r[:, :].rearrange("p (k c) -> p k c", k=KT)
            p = last_piece(c)
            if c == 0:
                return [(k8, w_in[:, :, VA0:VA0 + 256])]
            if p < PQA:
                k0 = 4 * (c - 1)
                return [(r[:, :].rearrange("p (k c) -> p k c", k=4), w_in[:, k0:k0 + 4, VA0 + 256:VA0 + 768])]
            if p < PVBC:
                n0 = 256 * (c - 3)
                return [(k8, w_in[:, :, n0:n0 + 256])]
            if p < PQB:
                k0 = 4 * (c - 9)
                v = r[:, 0:4 * VBC_N].rearrange("p (k c) -> p k c", k=4)
                return [(v[:, :, 0:128], w_in[:, k0:k0 + 4, VB0:VB0 + 128]),
                        (v[:, :, 128:VBC_N], w_in[:, k0:k0 + 4, VC0:VC0 + 260])]
            if c < 13:
                n0 = QB + 256 * (c - 11)
                return [(k8, w_in[:, :, n0:n0 + 256])]
            if c == 13:
                return [(r[:, 0:1024].rearrange("p (k c) -> p k c", k=KT), w_in[:, :, KB:KB + 128])]
            if c < 16:
                n0 = QC + 256 * (c - 14)
                return [(k8, w_in[:, :, n0:n0 + 256])]
            if PM <= p < PKX:
                k0 = 2 * (c - 32)
                return [(r[:, :].rearrange("p (k c) -> p k c", k=2), w_mix[:, k0:k0 + 2, :])]
            if p < PVX:
                return [(k8, w_xkv[:, :, 0:256])]
            if p < PXQ:
                return [(k8, w_xkv[:, :, 256:512])]
            if p < PXO:
                return [(k8, w_xq[:, :, :])]
            return [(r[:, :].rearrange("p (k c) -> p k c", k=2), w_xo[:, :, :])]

        CG, CM, CF, CO = 16, 32, 40, 40 + 2 * FF_PAIR
        arrivals = [0, 0]
        arrive_at = {}
        for c in range(CO + FF_PAIR):
            n_dma = 6 // 2 if CG <= c < CM and (c - CG) % 4 == 3 else len(chunk_loads(c)) if c < CG or CM <= c < CF else 1
            arrivals[c % 2] += 16 * n_dma
            arrive_at[c] = arrivals[c % 2]
        G_ARR = [32, 64]

        block = ctx.enter_context(nc.Block())

        @block.sync
        def _(sp):
            sp.dma_start(x_nat[:, 0, :], A["x"][0, 0:P, :]).then_inc(x_in[0], 16)
            sp.dma_start(raw[0][:, :].rearrange("p (k c) -> p k c", k=KT), chunk_loads(0)[0][1]).then_inc(raw_in[0], 16)
            for t in range(1, TT):
                sp.dma_start(x_nat[:, t, :], A["x"][0, t * P:(t + 1) * P, :]).then_inc(x_in[t], 16)

            def load(c):
                if c >= 2:
                    sp.wait_ge(lo_done, last_piece(c - 2) + 1)
                for dst, src in chunk_loads(c):
                    sp.dma_start(dst, src).then_inc(raw_in[c % 2], 16)

            for c in range(1, CG):
                load(c)
                if c == 3:
                    sp.dma_start(mem_nat[:, :, :], A["mem"][0].rearrange("(m p) n -> p m n", p=P)).then_inc(mem_in, 16)
            for i in range(N_PAIR):
                for q in range(4):
                    sp.wait_ge(lo_done, i * 8 + (PG + 2 * q - 2))
                    k8 = raw[q % 2][:, :].rearrange("p (k c) -> p k c", k=KT)
                    if q < 3:
                        n0 = GATES + q * D + i * 256
                        sp.dma_start(k8, w_in[:, :, n0:n0 + 256]).then_inc(raw_in[q % 2], 16)
                    else:
                        for w, (k0, k1) in zip(w_br, ((0, 2), (2, 6), (6, 8))):
                            sp.dma_start(k8[:, k0:k1, :], w[:, :, i * 256:(i + 1) * 256]).then_inc(raw_in[1], 16)
            for c in range(CM, CF):
                load(c)
                if c == CM:
                    sp.wait_ge(o_lo_done, KT)
                    sp.dma_start(resid[:, :, :], A["x"][0].rearrange("(t p) n -> p t n", p=P)).then_inc(resid_in, 16)
                    for i, w in enumerate(("ln1_g", "ln1_b")):
                        sp.dma_start(gb[:, i, :], A[w][0:1, :].to_broadcast([P, D])).then_inc(gb_in, 16)
            sp.wait_ge(gb_done, 2 * TT)
            for i, w in enumerate(("ln2_g", "ln2_b")):
                sp.dma_start(gb[:, i, :], A[w][0:1, :].to_broadcast([P, D])).then_inc(gb_in, 16)
            for i in range(FF_PAIR):
                for q in range(2):
                    sp.wait_ge(lo_done, i * 4 + (PF + 2 * q - 2))
                    n0 = i * 256 + q * D_FF
                    sp.dma_start(raw[q][:, :].rearrange("p (k c) -> p k c", k=KT),
                                 w_f1[:, :, n0:n0 + 256]).then_inc(raw_in[q], 16)
            sp.wait_ge(gb_done, 4 * TT)
            for i, w in enumerate(("ln3_g", "ln3_b")):
                sp.dma_start(gb[:, i, :], A[w][0:1, :].to_broadcast([P, D])).then_inc(gb_in, 16)
            for n in range(FF_PAIR):
                sp.wait_ge(lo_done, PO + 2 * n - 2)
                sp.dma_start(raw[n % 2][:, :].rearrange("p (k c) -> p k c", k=2),
                             w_f2[:, 2 * n:2 * n + 2, :]).then_inc(raw_in[n % 2], 16)
            for t in range(TT):
                sp.wait_ge(gb_done, 2 * (2 * TT + t + 1))
                sp.dma_start(out[0, t * P:(t + 1) * P, :], resid[:, t, :]).then_inc(stored, 16)
            sp.wait_ge(stored, 16 * TT)

        @block.gpsimd
        def _(pool):
            steps = 0
            for dst, src in ((b_rows[0:30, :], A["b_in"][0:1, 0:30 * P].rearrange("a (n p) -> (a n) p", p=P)),
                             (b_rows[30:54, :], A["b_in"][0:1, GATES:IN_W].rearrange("a (n p) -> (a n) p", p=P)),
                             (rel[:, :], A["rel_bias"]), (one_hot[:, :], A["one_hot"]), (seg_mask[:, :], A["seg_mask"]),
                             (bv[:, 0:768], A["b_in"][0:1, VA0:VA0 + 768].to_broadcast([P, 768])),
                             (bv[:, 768:896], A["b_in"][0:1, VB0:VB0 + 128].to_broadcast([P, 128])),
                             (bv[:, 896:1156], A["b_in"][0:1, VC0:VC0 + 260].to_broadcast([P, 260])),
                             (sink[:, :], A["attn_sinks"][0:1, :].to_broadcast([P, N_BH]))):
                pool.dma_start(dst, src).then_inc(small_in, 16)
            for m, v in ((ident, 0.0), (shift, 0.0), (spread, 0.0), (upper, 1.0), (causal, 0.0), (half, -0.5)):
                pool.memset(m[:, :], v).then_inc(pool_step, 1)
                steps += 1
            pool.wait_ge(pool_step, steps)
            pool.affine_select(out=ident[:, :], in_=ident[:, :], compare_op=ALU.not_equal, fill=1.0, base=0,
                               pattern=[[-1, P]], channel_multiplier=1).then_inc(const_ready, 1)
            pool.affine_select(out=shift[:, :], in_=shift[:, :], compare_op=ALU.not_equal, fill=1.0, base=384,
                               pattern=[[-1, 896]], channel_multiplier=1).then_inc(const_ready, 1)
            pool.affine_select(out=spread[:, :], in_=spread[:, :], compare_op=ALU.not_equal, fill=1.0, base=3,
                               pattern=[[-1, 516]], channel_multiplier=4).then_inc(const_ready, 1)
            pool.affine_select(out=upper[:, 0:P], in_=upper[:, 0:P], compare_op=ALU.is_ge, fill=0.0, base=0,
                               pattern=[[1, P]], channel_multiplier=-1).then_inc(const_ready, 1)
            pool.affine_select(out=causal[:, :], in_=causal[:, :], compare_op=ALU.is_ge, fill=MASK, base=0,
                               pattern=[[-1, P]], channel_multiplier=1).then_inc(const_ready, 1)
            pool.wait_ge(seg_ready, 3)
            copies = ((rows1, 0, 0, N_AH, 0, SEG1), (rows1, N_AH, N_G * N_AH, N_BH, 0, SEG1),
                      (rows4, 0, N_AH, N_AH, SEG1, SEG4), (rows16, 0, 2 * N_AH, N_AH, SEG1 + SEG4, SEG16))
            for rows, to, h0, nh, at, width in copies:
                pool.dma_start(rows.ap()[to:to + nh, :, :],
                               seg_row[h0:h0 + nh, at:at + width].unsqueeze(1).broadcast_to([nh, P, width])).then_inc(seg_out, 16)
            pool.wait_ge(seg_out, 16 * len(copies))
            pool.wait_ge(mem_turned, 4)
            for tab, rows, nh, width, cols in ((tab1, rows1, N_AH + N_BH, SEG1, 256), (tab4, rows4, N_AH, SEG4, P),
                                               (tab16, rows16, N_AH, SEG16, P)):
                for h in range(nh):
                    pool.dma_start(tab[:, h, :], bass.AP(rows, h * P * width + P - 1, [[width - 1, P], [1, cols]])).then_inc(table_in, 16)

            def scale_probs(j):
                for banks in JOBS[j][0]:
                    for kind, h, t, _, cols, at in banks:
                        buf = probx if kind == "X" else prob
                        if kind == "A0":
                            f = factor[:, t, 0, h:h + 1]
                        elif kind in ("A1", "A2"):
                            f = factor_s[:, 0 if kind == "A1" else 1, t, h:h + 1]
                        else:
                            n = stat_col(kind, h, t)
                            f = rsum[:, n:n + 1]
                        v = buf[:, SLOT(j), at:at + cols]
                        pool.tensor_scalar(v, v, f, None, ALU.mult).then_inc(prob_ready, 1)

            def mask_diagonals(j):
                for kind, h, t, _, cols, at in sorted(sum(JOBS[j][0], []), key=lambda u: u[2]):
                    pool.wait_ge(base_ready, TT * (j - 8) + t + 1)
                    v = prob[:, SLOT(j), at + cols - P:at + cols]
                    pool.tensor_tensor(v, v, causal[:, :], ALU.add).then_inc(diag_ready, 1)

            pool.wait_ge(factor_ready, 2)
            for j in range(N_AH):
                scale_probs(j)
            for j in range(4, N_SELF):
                if j >= 8:
                    mask_diagonals(j)
                pool.wait_ge(rsum_ready, j - 4 + 1)
                scale_probs(j)

            nonlocal_steps = [steps]

            def norm(first):
                for t in range(TT):
                    pool.wait_ge(var_done, first + t + 1)
                    pool.tensor_scalar(rstd[:, t, 0:1], mv[:, t, 1:2], LN_EPS, None, ALU.add).then_inc(pool_step, 1)
                    nonlocal_steps[0] += 1
                    pool.wait_ge(pool_step, nonlocal_steps[0])
                    pool.tensor_tensor(rstd[:, t, 1:2], rstd[:, t, 0:1], half[:, 0:1], ALU.pow).then_inc(pool_step, 1)
                    nonlocal_steps[0] += 1
                    pool.wait_ge(pool_step, nonlocal_steps[0])
                    pool.tensor_scalar(rstd[:, t, 2:3], mv[:, t, 0:1], rstd[:, t, 1:2], -1.0, ALU.mult, ALU.mult).then_inc(rstd_done, 1)
                    if t >= 1:
                        gain(first, t - 1)
                gain(first, TT - 1)

            def gain(first, t):
                if t == 0:
                    pool.wait_ge(gb_in, 32 * (first // TT + 1))
                pool.wait_ge(norm_done, first + t + 1)
                v = resid[:, t, :]
                pool.tensor_tensor(v, v, gb[:, 0, :], ALU.mult).then_inc(gb_done, 1)
                pool.wait_ge(gb_done, 2 * (first + t) + 1)
                pool.tensor_tensor(v, v, gb[:, 1, :], ALU.add).then_inc(gb_done, 1)

            norm(0)
            for j in range(N_SELF, N_JOB):
                pool.wait_ge(rsum_ready, j - 4 + 1)
                scale_probs(j)
            norm(TT)
            norm(2 * TT)

        @block.scalar
        def _(act):
            def split(p):
                c = chunk_of(p)
                act.wait_ge(raw_in[c % 2], arrive_at[c])
                if p >= 2:
                    act.wait_ge(piece_done, p - 1)
                src, hi, _ = raw_piece(p)
                act.copy(hi, src).then_inc(hi_done, 1)

            def turn_drain(n, count):
                t, hf = n // 2, n % 2
                act.wait_ge(turned, count + 1)
                act.copy(xt_hi[:, 4 * hf:4 * hf + 4, t * P:(t + 1) * P],
                         ps[:, 2 * t + hf, :].rearrange("p (k c) -> p k c", k=4)).then_inc(turn_hi, 1)

            def exps(j, lo, hi):
                units = sum(JOBS[j][0], [])
                for u in range(lo, min(hi, len(units))):
                    kind, h, t, _, cols, at = units[u]
                    buf = probx if kind == "X" else prob
                    if kind[0] == "A":
                        g = int(kind[1])
                        nm, dn = stat_a[:, t, g, 0, h:h + 1], stat_a[:, t, g, 1, h:h + 1]
                    else:
                        c = stat_col(kind, h, t)
                        nm, dn = nmax[:, c:c + 1], psum_[:, c:c + 1]
                    act.wait_ge(neg_ready, units_before[j] + u + 1)
                    v = buf[:, SLOT(j), at:at + cols]
                    act.activation(v, v, ACT.Exp, bias=nm, scale=-1.0, accum_out=dn).then_inc(exp_done, 1)
                if hi >= len(units) and kind == "B":
                    for hh in (units[0][1], units[0][1] + 1):
                        act.activation(esink[:, hh * TT:(hh + 1) * TT], nmax[:, hh * TT:(hh + 1) * TT], ACT.Exp,
                                       bias=sink[:, hh:hh + 1]).then_inc(esink_done, 1)

            def fox_base(j):
                h = j - 8
                act.wait_ge(ncum_ps, h + 1)
                for t in range(TT):
                    n = (t + 1) * P
                    act.activation(prob[:, SLOT(j), C_AT[t]:C_AT[t] + n], ps[:, 3, 0:n], ACT.Identity,
                                   bias=cum[:, t, h:h + 1]).then_inc(base_ready, 1)

            def pt_drain(j):
                for g in range(len(JOBS[j][1])):
                    n = group_index[(j, g)]
                    if n % 2 == 0:
                        act.wait_ge(pt_ps, n + 1)
                        if n >= PT_SLOTS:
                            act.wait_ge(av_done, n - PT_SLOTS + 1)
                        w = P * len(JOBS[j][1][g][0])
                        dst = ptx if j >= N_SELF else pt
                        act.copy(dst[:, n % PT_SLOTS, 0:w], ps[:, 4 + n % 2, 0:w]).then_inc(pt_act, 1)
                    for m in accs_after[j]:
                        if acc_end[m] == n - 1:
                            acc_drain(m)
                for m in accs_after[j]:
                    if acc_end[m] == group_index[(j, len(JOBS[j][1]) - 1)]:
                        acc_drain(m)

            def acc_drain(m):
                kind, h = acc_kind[m]
                half_ = slice(64 * (h % 2), 64 * (h % 2) + 64)
                if acc_by_dve[m]:
                    return
                act.wait_ge(av_done, acc_end[m] + 1)
                src = ps[half_, 6 + m % 2, :]
                if kind == "X":
                    act.copy(ox_hi[half_, h // 2, :], src).then_inc(acc_act, 1)
                    return
                tile = {"A0": 0, "B": 12, "C": 18}[kind] + h // 2
                act.copy(qk[half_, tile, :], src).then_inc(acc_act, 1)

            act.wait_ge(const_ready, 5)
            for n in range(2 * TT):
                turn_drain(n, n)
                if n == 1:
                    split(0)
            for p in range(0, 18):
                split(p + 1)
                if p == PQA + 3:
                    for n in range(4):
                        act.wait_ge(mem_turned, n + 1)
                        m, hf = n // 2, n % 2
                        act.copy(memt_hi[:, 4 * hf:4 * hf + 4, m * P:(m + 1) * P],
                                 ps[:, 2 + n, :].rearrange("p (k c) -> p k c", k=4)).then_inc(mem_hi, 1)
            for what, n in FRONT:
                if what == "scores":
                    exps(n, 0, 99)
                elif what == "piece":
                    split(n + 1)
                    if n == 22:
                        act.wait_ge(abs_ready, 1)
                        act.activation(fl[:, 1, :, :], fl[:, 0, :, :], ACT.Exp).then_inc(act_f, 1)
                        act.wait_ge(act_f, 1)
                        act.activation(fl[:, 2, :, :], fl[:, 1, :, :], ACT.Ln, bias=1.0).then_inc(act_f, 1)
                elif what == "forward":
                    act.wait_ge(diff_ready, 1)
                    act.activation(comb_e[:, :, :, :], comb_e[:, :, :, :], ACT.Exp).then_inc(comb_exp, 1)
            for what, n in BACKHALF:
                if what == "output":
                    pt_drain(n)
                else:
                    if n >= 8:
                        fox_base(n)
                    exps(n, 0, 99)
            for m, tile in enumerate(OUT_TILES):
                if m == 0:
                    act.wait_ge(av_done, groups_before[N_SELF])
                    act.wait_ge(acc_dve, N_AH)
                    act.wait_ge(acc_act, c_act - N_XH)
                act.copy(o_hi[:, m, :], qk[:, tile, :]).then_inc(o_hi_done, 1)
            act.wait_ge(o_lo_done, KT)

            def gate_iteration(i, last):
                for q in range(8):
                    p = PG + q
                    np_, wrap = (p + 1, 0) if q < 7 else (PG, 1)
                    if last and q == 7:
                        split(PM)
                    else:
                        gate_split(i, np_ - PG, wrap)
                    if q < 6:
                        br, b = q // 2, q % 2
                        act.wait_ge(piece_done, i * 8 + (p + 1))
                        act.activation(sg[:, q, :], ps[:, q, :], ACT.Sigmoid,
                                       bias=bias_t[:, bass.ds(i * 2 + (30 + 8 * br + b), 1)]).then_inc(sig_done, 1)

            def gate_split(i, q, wrap):
                p = PG + q
                c = q // 2
                slot = c % 2
                base = arrive_at[CG - 2 + slot]
                within = {0: 16, 1: 16, 2: 32, 3: 64}[c]
                act.wait_ge(raw_in[slot], (i + wrap) * G_ARR[slot] + (base + within))
                act.wait_ge(piece_done, (i + wrap) * 8 + (p - 1))
                v = raw[slot][:, :].rearrange("p (k c) -> p k c", k=KT)[:, :, (q % 2) * P:(q % 2 + 1) * P]
                act.copy(w_hi[p % 2][:, :].rearrange("p (k c) -> p k c", k=KT), v).then_inc(hi_done, 1)

            with act.Fori(0, N_PAIR - 1) as i:
                gate_iteration(i, False)
            gate_iteration(N_PAIR - 1, True)
            for p in range(PM, PXQ):
                if p + 1 < PXQ:
                    split(p + 1)

            def norm(first):
                for t in range(TT):
                    act.wait_ge(rstd_done, first + t + 1)
                    act.activation(resid[:, t, :], resid[:, t, :], ACT.Identity, bias=rstd[:, t, 2:3],
                                   scale=rstd[:, t, 1:2]).then_inc(norm_done, 1)
                    if t >= 1 and first < 2 * TT:
                        for hf in range(2):
                            turn_drain(2 * (t - 1) + hf, 2 * (first + TT + t - 1) + hf)
                if first < 2 * TT:
                    for hf in range(2):
                        turn_drain(2 * (TT - 1) + hf, 2 * (first + TT + TT - 1) + hf)

            norm(0)
            split(PXQ)
            split(PXQ + 1)
            split(PXO)
            for j in range(N_SELF, N_JOB):
                exps(j, 0, 99)
                if j >= N_SELF + 2:
                    pt_drain(j - 2)
            split(PXO + 1)
            pt_drain(N_JOB - 2)
            pt_drain(N_JOB - 1)
            norm(TT)

            F_BASE = [arrive_at[CF - 2], arrive_at[CF - 1]]

            def ffn_split(i, q, wrap):
                p = PF + q
                slot = (q // 2) % 2
                act.wait_ge(raw_in[slot], (i + wrap) * 16 + (F_BASE[slot] + 16))
                act.wait_ge(piece_done, (i + wrap) * 4 + (p - 1))
                v = raw[slot][:, :].rearrange("p (k c) -> p k c", k=KT)[:, :, (q % 2) * P:(q % 2 + 1) * P]
                act.copy(w_hi[p % 2][:, :].rearrange("p (k c) -> p k c", k=KT), v).then_inc(hi_done, 1)

            def ffn_iteration(i, last):
                for q in range(4):
                    if last and q == 3:
                        out_split(0)
                    else:
                        ffn_split(i, (q + 1) % 4, (q + 1) // 4)
                    if q < 2:
                        act.wait_ge(piece_done, i * 4 + (PF + q + 1))
                        act.wait_ge(h_done, i * 2)
                        act.activation(sa[:, q, :], ps[:, q, :], ACT.Silu).then_inc(silu_done, 1)

            def out_split(n):
                p = PO + n
                act.wait_ge(raw_in[(n // 2) % 2], arrive_at[CO + n // 2])
                act.wait_ge(piece_done, p - 1)
                act.copy(w_hi[p % 2][:, :], raw[(n // 2) % 2][:, (n % 2) * 1024:(n % 2 + 1) * 1024]).then_inc(hi_done, 1)

            ffn_split(0, 0, 0)
            with act.Fori(0, FF_PAIR - 1) as i:
                ffn_iteration(i, False)
            ffn_iteration(FF_PAIR - 1, True)
            for n in range(1, FF_T):
                out_split(n)
            norm(2 * TT)

        @block.vector
        def _(dve):
            chain = [0]

            def link(ins):
                chain[0] += 1
                ins.then_inc(dve_step, 1)
                dve.wait_ge(dve_step, chain[0])

            def f32(ap):
                return ap.bitcast(F32)

            def rest_of(p):
                dve.wait_ge(hi_done, p + 1)
                src, hi, lo = raw_piece(p)
                dve.tensor_tensor(lo, src, f32(hi), ALU.subtract).then_inc(lo_done, 1)

            def turn_drain(n, count):
                t, hf = n // 2, n % 2
                dve.wait_ge(turn_hi, count + 1)
                at = (slice(None), slice(4 * hf, 4 * hf + 4), slice(t * P, (t + 1) * P))
                dve.tensor_tensor(xt_lo[at], ps[:, 2 * t + hf, :].rearrange("p (k c) -> p k c", k=4),
                                  f32(xt_hi[at]), ALU.subtract).then_inc(turn_lo, 1)

            def split3(dst, src, tmp):
                link(dve.tensor_copy(dst[:, 0, :], src))
                link(dve.tensor_tensor(tmp, src, dst[:, 0, :], ALU.subtract))
                link(dve.tensor_copy(dst[:, 1, :], tmp))
                link(dve.tensor_tensor(tmp, tmp, dst[:, 1, :], ALU.subtract))
                return dve.tensor_copy(dst[:, 2, :], tmp)

            def strided(bank):
                return ps[:, bank, :].rearrange("p (i s) -> p s i", s=4)

            def drain_piece(p):
                if p == PV0 + 1:
                    dve.wait_ge(piece_done, p + 1)
                    for b in range(2):
                        dve.tensor_tensor(va[:, 2 * b:2 * b + 2, 0:256], ps[:, b, :].rearrange("p (t c) -> p t c", t=2),
                                          bv[:, 0:256].unsqueeze(1).broadcast_to([P, 2, 256]), ALU.add).then_inc(proj_out, 1)
                elif p == PV12 + 3:
                    dve.wait_ge(piece_done, p + 1)
                    for t in range(TT):
                        dve.tensor_tensor(va[:, t, 256:768], ps[:, 2 + t, :], bv[:, 256:768], ALU.add).then_inc(proj_out, 1)
                elif PQA <= p < PVBC:
                    n = p - PQA
                    dve.wait_ge(piece_done, p + 1)
                    bank = (6, 7, 0, 1)[n % 4]
                    scale = SCALE if n < 6 else 1.0
                    if n % 6 < 2:
                        dst, src = qk[:, n, :], ps[:, bank, :]
                    else:
                        dst, src = qk[:, n, :].rearrange("p (s i) -> p s i", s=4), strided(bank)
                    dve.tensor_scalar(dst, src, bias_t[:, n:n + 1], scale, ALU.add, ALU.mult).then_inc(proj_out, 1)
                elif p == PVBC + 3:
                    dve.wait_ge(piece_done, p + 1)
                    for t in range(TT):
                        dve.tensor_tensor(vbc[:, t, :], ps[:, 4 + t, 0:VBC_N], bv[:, 768:768 + VBC_N], ALU.add).then_inc(proj_out, 1)
                    dve.wait_ge(proj_out, 18 + 4)
                    dve.scalar_tensor_tensor(out=fl[:, 0, :, :], in0=vbc[:, :, 384:388], scalar=-1.0,
                                             in1=vbc[:, :, 384:388], op0=ALU.mult, op1=ALU.min).then_inc(abs_ready, 1)
                elif PQB <= p < PG:
                    n = p - PQB
                    dve.wait_ge(piece_done, p + 1)
                    bank = 4 + n % 4
                    if n == 4:
                        for kv in range(2):
                            for hf in range(2):
                                ins = dve.tensor_scalar(qk[64 * hf:64 * hf + 64, T_KB + kv, :], ps[64 * kv:64 * kv + 64, bank, :],
                                                        bias_t[64 * kv:64 * kv + 64, 22:23], 1.0, ALU.add, ALU.mult)
                        ins.then_inc(proj_out, 1)
                    else:
                        tile, col, scale = ((T_QB + n, 18 + n, SCALE) if n < 4 else
                                            (T_QC + n - 5, 24 + n - 5, SCALE if n < 7 else 1.0))
                        dve.tensor_scalar(qk[:, tile, :], ps[:, bank, :], bias_t[:, col:col + 1], scale,
                                          ALU.add, ALU.mult).then_inc(proj_out, 1)

            def scores_out(j):
                for b, units in enumerate(JOBS[j][0]):
                    dve.wait_ge(score_ps, bank_index[(j, b)] + 1)
                    bank = score_bank(j, b)
                    for kind, h, t, c0, cols, at in units:
                        buf = probx if kind == "X" else prob
                        dst = buf[:, SLOT(j), at:at + cols]
                        start = HUGE
                        if kind == "A0":
                            bias, nm = tab1[:, h, 256 - cols:256], stat_a[:, t, 0, 0, h:h + 1]
                        elif kind == "A1":
                            bias, nm = tab4[:, h, :], stat_a[:, t, 1, 0, h:h + 1]
                        elif kind == "A2":
                            bias, nm = tab16[:, h, :], stat_a[:, t, 2, 0, h:h + 1]
                        else:
                            c = stat_col(kind, h, t)
                            nm = nmax[:, c:c + 1]
                            if kind == "B":
                                bias, start = tab1[:, N_AH + h, 256 - cols:256], neg_sink[:, h:h + 1]
                            elif kind == "C":
                                dve.wait_ge(diag_ready, TT * h + t + 1)
                                bias = dst
                            else:
                                bias = zero[:, 0:cols]
                        dve.tensor_tensor_reduce(dst, ps[:, bank, c0:c0 + cols], bias, -1.0, start, ALU.add, ALU.min,
                                                 nm).then_inc(neg_ready, 1)

            def sums_out(j):
                kind = JOBS[j][1][0][2]
                h0 = JOBS[j][1][0][3]
                nh = 2 if kind == "B" else 1
                c = stat_col(kind, h0, 0)
                v = slice(c, c + nh * TT)
                dve.wait_ge(exp_done, units_before[j + 1])
                if kind == "B":
                    dve.wait_ge(esink_done, h0 + 2)
                    link(dve.tensor_tensor(psum_[:, v], psum_[:, v], esink[:, v], ALU.add))
                dve.reciprocal(rsum[:, v], psum_[:, v]).then_inc(rsum_ready, 1)

            def pt_drain(j):
                for g in range(len(JOBS[j][1])):
                    n = group_index[(j, g)]
                    if n % 2 == 1:
                        dve.wait_ge(pt_ps, n + 1)
                        if n >= PT_SLOTS:
                            dve.wait_ge(av_done, n - PT_SLOTS + 1)
                        w = P * len(JOBS[j][1][g][0])
                        dst = ptx if j >= N_SELF else pt
                        dve.tensor_copy(dst[:, n % PT_SLOTS, 0:w], ps[:, 4 + n % 2, 0:w]).then_inc(pt_dve, 1)
                for m in accs_after[j]:
                    acc_drain(m)

            def acc_drain(m):
                kind, h = acc_kind[m]
                half_ = slice(64 * (h % 2), 64 * (h % 2) + 64)
                if kind == "X":
                    dve.wait_ge(acc_act, acc_count[m])
                    dve.tensor_tensor(ox_lo[half_, h // 2, :], ps[half_, 6 + m % 2, :], f32(ox_hi[half_, h // 2, :]),
                                      ALU.subtract).then_inc(oxl_done, 1)
                elif acc_by_dve[m]:
                    dve.wait_ge(av_done, acc_end[m] + 1)
                    dve.wait_ge(acc_act, acc_count[m - 1])
                    o = qk[half_, h // 2, :].rearrange("p (i s) -> p i s", s=4)
                    dve.tensor_tensor(o, ps[half_, 6 + m % 2, :].rearrange("p (s i) -> p i s", s=4), o,
                                      ALU.add).then_inc(acc_dve, 1)

            for n in range(2 * TT):
                turn_drain(n, n)
            rest_of(0)
            dve.wait_ge(seg_ps, 3)
            dve.wait_ge(small_in, 16 * 9)
            dve.tensor_copy(bias_t[:, :], ps[:, 6, 448:502]).then_inc(seg_ready, 1)
            dve.tensor_tensor(seg_row[:, 0:SEG_CUT], ps[0:N_BIAS, 7, 0:SEG_CUT], seg_mask[:, 0:SEG_CUT], ALU.add).then_inc(seg_ready, 1)
            dve.tensor_tensor(seg_row[:, SEG_CUT:SEG_N], ps[0:N_BIAS, 6, 0:SEG_N - SEG_CUT], seg_mask[:, SEG_CUT:SEG_N],
                              ALU.add).then_inc(seg_ready, 1)
            link(dve.tensor_scalar(neg_sink[:, :], sink[:, :], -1.0, None, ALU.mult))
            dve.wait_ge(seg_ready, 1)
            for p in range(0, 18):
                rest_of(p + 1)
                drain_piece(p)
                if p == PQA + 3:
                    for n in range(4):
                        m, hf = n // 2, n % 2
                        dve.wait_ge(mem_hi, n + 1)
                        at = (slice(None), slice(4 * hf, 4 * hf + 4), slice(m * P, (m + 1) * P))
                        dve.tensor_tensor(memt_lo[at], ps[:, 2 + n, :].rearrange("p (k c) -> p k c", k=4),
                                          f32(memt_hi[at]), ALU.subtract).then_inc(mem_lo, 1)
            dve.wait_ge(table_in, 16 * (N_AH + N_BH + 2 * N_AH))
            for what, n in FRONT:
                if what == "scores":
                    scores_out(n)
                elif what == "piece":
                    if n + 1 < PG:
                        rest_of(n + 1)
                    drain_piece(n)
                    if n == 23:
                        dve.wait_ge(act_f, 2)
                        dve.scalar_tensor_tensor(out=logf[:, :, :], in0=vbc[:, :, 384:388], scalar=0.0, in1=fl[:, 2, :, :],
                                                 op0=ALU.min, op1=ALU.subtract).then_inc(dve_step, 1)
                        chain[0] += 1
                        dve.wait_ge(dve_step, chain[0])
                        split3(lparts, logf[:, :, :].rearrange("p t h -> p (t h)"),
                               fl[:, 0, :, :].rearrange("p t h -> p (t h)")).then_inc(lparts_ready, 1)
                    if n == 27:
                        dve.wait_ge(exp_done, units_before[N_AH])
                        split3(parts, stat_a[:, :, :, :, :].rearrange("p t g d h -> p (t g d h)"), rest[:, :]).then_inc(parts_ready, 1)
                elif what == "forward":
                    dve.wait_ge(cum_ps, 1)
                    link(dve.tensor_copy(cum3[:, :, :, :].rearrange("p t c h -> p (t c h)"), ps[:, 1, 0:48]))
                    link(dve.tensor_tensor(cum[:, :, :], cum3[:, :, 0, :], cum3[:, :, 1, :], ALU.add))
                    dve.tensor_tensor(cum[:, :, :], cum[:, :, :], cum3[:, :, 2, :], ALU.add).then_inc(cum_ready, 1)
                    dve.wait_ge(moved_ps, 1)
                    link(dve.tensor_copy(moved[:, :], ps[:, 0, 0:192]))
                    mvw = moved[:, :].rearrange("p (t g c x) -> p t g c x", t=TT, g=2, c=3)
                    nat = stat_nat[:, :, :, :, :].rearrange("p t g d h -> p t g (d h)")
                    link(dve.tensor_copy(nat[:, :, 0, :], stat_a[:, :, 0, :, :].rearrange("p t d h -> p t (d h)")))
                    link(dve.tensor_tensor(nat[:, :, 1:3, :], mvw[:, :, :, 0, :], mvw[:, :, :, 1, :], ALU.add))
                    link(dve.tensor_tensor(nat[:, :, 1:3, :], nat[:, :, 1:3, :], mvw[:, :, :, 2, :], ALU.add))
                    nm = [stat_nat[:, :, g, 0, :] for g in range(3)]
                    link(dve.tensor_tensor(comb_min[:, :, :], nm[0], nm[1], ALU.min))
                    link(dve.tensor_tensor(comb_min[:, :, :], comb_min[:, :, :], nm[2], ALU.min))
                    dve.tensor_tensor(comb_e[:, :, :, :], comb_min[:, :, :].unsqueeze(2).broadcast_to([P, TT, N_G, N_AH]),
                                      stat_nat[:, :, :, 0, :], ALU.subtract).then_inc(diff_ready, 1)
                    dve.wait_ge(comb_exp, 1)
                    link(dve.tensor_tensor(comb_z[:, :, :, :], comb_e[:, :, :, :], stat_nat[:, :, :, 1, :], ALU.mult))
                    link(dve.tensor_tensor(comb_min[:, :, :], comb_z[:, :, 0, :], comb_z[:, :, 1, :], ALU.add))
                    link(dve.tensor_tensor(comb_min[:, :, :], comb_min[:, :, :], comb_z[:, :, 2, :], ALU.add))
                    link(dve.reciprocal(comb_min[:, :, :], comb_min[:, :, :]))
                    link(dve.tensor_tensor(factor[:, :, :, :], comb_e[:, :, :, :],
                                           comb_min[:, :, :].unsqueeze(2).broadcast_to([P, TT, N_G, N_AH]), ALU.mult))
                    dve.wait_ge(moved_ps, 1)
                    split3(parts[:, :, 0:48], factor[:, :, :, :].rearrange("p t g h -> p (t g h)"),
                           rest[:, 0:48]).then_inc(fparts_ready, 1)
                elif what == "back":
                    dve.wait_ge(cumt_ps, 1)
                    dve.tensor_scalar(ncum_t[:, :], ps[0:N_CH, 3, :], -1.0, None, ALU.mult).then_inc(cumt_out, 1)
                    dve.wait_ge(back_ps, 1)
                    link(dve.tensor_copy(moved[:, 0:96], ps[:, 2, 0:96]))
                    msw = moved[:, 0:96].rearrange("p (g s c h) -> p g s c h", g=2, s=TT, c=3)
                    for g in range(2):
                        link(dve.tensor_tensor(factor_s[:, g, :, :], msw[:, g, :, 0, :], msw[:, g, :, 1, :], ALU.add))
                        dve.tensor_tensor(factor_s[:, g, :, :], factor_s[:, g, :, :], msw[:, g, :, 2, :], ALU.add).then_inc(factor_ready, 1)
            for what, n in BACKHALF:
                if what == "output":
                    pt_drain(n)
                    if 4 <= n + 3 < N_SELF:
                        sums_out(n + 3)
                else:
                    scores_out(n)
            rest_of(PG)
            for m, tile in enumerate(OUT_TILES):
                dve.wait_ge(o_hi_done, m + 1)
                dve.tensor_tensor(o_lo[:, m, :], qk[:, tile, :], f32(o_hi[:, m, :]), ALU.subtract).then_inc(o_lo_done, 1)

            def gate_rest(i, q, wrap):
                p = PG + q
                slot = (q // 2) % 2
                dve.wait_ge(hi_done, (i + wrap) * 8 + (p + 1))
                v = raw[slot][:, :].rearrange("p (k c) -> p k c", k=KT)[:, :, (q % 2) * P:(q % 2 + 1) * P]
                s = p % 2
                dve.tensor_tensor(w_lo[s][:, :].rearrange("p (k c) -> p k c", k=KT), v,
                                  f32(w_hi[s][:, :]).rearrange("p (k c) -> p k c", k=KT), ALU.subtract).then_inc(lo_done, 1)

            MERGE_STEPS = 6

            def gate_iteration(i, last):
                for q in range(8):
                    if last and q == 7:
                        rest_of(PM)
                    else:
                        gate_rest(i, (q + 1) % 8, (q + 1) // 8)
                    if q >= 6:
                        b = q - 6
                        dve.wait_ge(piece_done, i * 8 + (PG + q + 1))
                        dve.wait_ge(sig_done, i * 6 + 6)
                        banks = (6, 7, 0) if b == 0 else (1, 2, 3)
                        at = bass.ds(i * 1024 + b * 512, 512)
                        mh = m_hi[:, :, :].rearrange("p k c -> p (k c)")[:, at]
                        ml = m_lo[:, :, :].rearrange("p k c -> p (k c)")[:, at]
                        step = lambda n: i * (2 * MERGE_STEPS) + (b * MERGE_STEPS + n)
                        dve.wait_ge(merge_step, step(0))
                        dve.tensor_tensor(mt[:, 0, :], ps[:, banks[0], :], sg[:, b, :], ALU.mult).then_inc(merge_step, 1)
                        dve.tensor_tensor(mt[:, 1, :], ps[:, banks[1], :], sg[:, 2 + b, :], ALU.mult).then_inc(merge_step, 1)
                        dve.tensor_tensor(mt[:, 2, :], ps[:, banks[2], :], sg[:, 4 + b, :], ALU.mult).then_inc(
                            merged_even if b == 0 else merged_odd, 1)
                        dve.wait_ge(merge_step, step(2))
                        dve.tensor_tensor(mt[:, 0, :], mt[:, 0, :], mt[:, 1, :], ALU.add).then_inc(merge_step, 1)
                        dve.wait_ge(merge_step, step(3))
                        dve.wait_ge(merged_even if b == 0 else merged_odd, i + 1)
                        dve.tensor_tensor(mt[:, 0, :], mt[:, 0, :], mt[:, 2, :], ALU.add).then_inc(merge_step, 1)
                        dve.wait_ge(merge_step, step(4))
                        dve.tensor_copy(mh, mt[:, 0, :]).then_inc(merge_step, 1)
                        dve.wait_ge(merge_step, step(5))
                        dve.tensor_tensor(ml, mt[:, 0, :], f32(mh), ALU.subtract).then_inc(merge_step, 1)

            with dve.Fori(0, N_PAIR - 1) as i:
                gate_iteration(i, False)
            gate_iteration(N_PAIR - 1, True)

            def rows_out(first, t, ready):
                ready()
                if t == 0 and first == 0:
                    dve.wait_ge(resid_in, 16)
                for n in range(2):
                    v = resid[:, t, n * 512:(n + 1) * 512]
                    dve.scalar_tensor_tensor(out=v, in0=v, scalar=ALPHA, in1=ps[:, 2 * t + n, :], op0=ALU.mult,
                                             op1=ALU.add).then_inc(y_done, 1)
                for n in range(2):
                    dve.wait_ge(y_done, 2 * (first + t) + n + 1)
                    ins = dve.bn_stats(bn[:, t, n, :], resid[:, t, n * 512:(n + 1) * 512])
                    if n == 1:
                        link(ins)
                    else:
                        ins.then_inc(dve_step, 1)
                        chain[0] += 1
                dve.bn_aggr(mv[:, t, :], bn[:, t, :, :].rearrange("p a b -> p (a b)")).then_inc(var_done, 1)

            def norm_phase(first, last_p):
                for t in range(TT):
                    if t < TT - 1:
                        rows_out(first, t, lambda: dve.wait_ge(rows_done, (first // TT) * (TT - 1) + t + 1))
                    else:
                        rows_out(first, t, lambda: dve.wait_ge(piece_done, last_p + 1))

            for p in range(PM, PM + 7):
                rest_of(p + 1)
            rows_out(0, 0, lambda: dve.wait_ge(rows_done, 1))
            rest_of(PKX)
            rows_out(0, 1, lambda: dve.wait_ge(rows_done, 2))
            rest_of(PKX + 1)
            rows_out(0, 2, lambda: dve.wait_ge(rows_done, 3))
            rows_out(0, 3, lambda: dve.wait_ge(piece_done, PM + 8))
            dve.memset(zero[:, :], 0.0).then_inc(zero_ready, 1)
            for n in range(2):
                rest_of(PVX + n)
                dve.wait_ge(piece_done, PKX + n + 1)
                dve.tensor_copy(kx[:, n, :], ps[:, n, 0:MEM]).then_inc(memkv_out, 1)
            dve.wait_ge(piece_done, PVX + 2)
            dve.tensor_copy(vx[:, :, :], ps[:, 2, :].rearrange("p (m c) -> p m c", m=2)).then_inc(memkv_out, 1)
            for n in range(2 * TT):
                turn_drain(n, 2 * TT + n)
            rest_of(PXQ)
            rest_of(PXQ + 1)
            for n in range(2):
                dve.wait_ge(piece_done, PXQ + n + 1)
                dve.tensor_scalar(qx[:, n, :], ps[:, n, :], SCALE, None, ALU.mult).then_inc(xq_out, 1)
            rest_of(PXO)
            dve.wait_ge(zero_ready, 1)
            for j in range(N_SELF, N_JOB):
                scores_out(j)
                if j >= N_SELF + 1:
                    sums_out(j - 1)
                if j >= N_SELF + 2:
                    pt_drain(j - 2)
            sums_out(N_JOB - 1)
            rest_of(PXO + 1)
            pt_drain(N_JOB - 2)
            pt_drain(N_JOB - 1)
            norm_phase(TT, PXO + 1)
            for n in range(2 * TT):
                turn_drain(n, 4 * TT + n)

            def ffn_rest(i, q, wrap):
                p = PF + q
                slot, s = (q // 2) % 2, p % 2
                dve.wait_ge(hi_done, (i + wrap) * 4 + (p + 1))
                v = raw[slot][:, :].rearrange("p (k c) -> p k c", k=KT)[:, :, (q % 2) * P:(q % 2 + 1) * P]
                dve.tensor_tensor(w_lo[s][:, :].rearrange("p (k c) -> p k c", k=KT), v,
                                  f32(w_hi[s][:, :]).rearrange("p (k c) -> p k c", k=KT), ALU.subtract).then_inc(lo_done, 1)

            def out_rest(n):
                p = PO + n
                dve.wait_ge(hi_done, p + 1)
                dve.tensor_tensor(w_lo[p % 2][:, :], raw[(n // 2) % 2][:, (n % 2) * 1024:(n % 2 + 1) * 1024],
                                  f32(w_hi[p % 2][:, :]), ALU.subtract).then_inc(lo_done, 1)

            def ffn_iteration(i, last):
                for q in range(4):
                    if last and q == 3:
                        out_rest(0)
                    else:
                        ffn_rest(i, (q + 1) % 4, (q + 1) // 4)
                    if q >= 2:
                        b = q - 2
                        dve.wait_ge(piece_done, i * 4 + (PF + q + 1))
                        dve.wait_ge(silu_done, i * 2 + (b + 1))
                        at = bass.ds(i * 1024 + b * 512, 512)
                        hh = h_hi[:, :, :].rearrange("p k c -> p (k c)")[:, at]
                        hl = h_lo[:, :, :].rearrange("p k c -> p (k c)")[:, at]
                        dve.wait_ge(ffn_step, i * 4 + 2 * b)
                        dve.wait_ge(h_done, i * 2 + b)
                        dve.tensor_tensor(ht[:, :], ps[:, 2 + b, :], sa[:, b, :], ALU.mult).then_inc(ffn_step, 1)
                        dve.wait_ge(ffn_step, i * 4 + (2 * b + 1))
                        dve.tensor_copy(hh, ht[:, :]).then_inc(ffn_step, 1)
                        dve.wait_ge(ffn_step, i * 4 + (2 * b + 2))
                        dve.tensor_tensor(hl, ht[:, :], f32(hh), ALU.subtract).then_inc(h_done, 1)

            ffn_rest(0, 0, 0)
            with dve.Fori(0, FF_PAIR - 1) as i:
                ffn_iteration(i, False)
            ffn_iteration(FF_PAIR - 1, True)
            for n in range(1, FF_T):
                out_rest(n)
            norm_phase(2 * TT, P_END - 1)

        @block.tensor
        def _(pe):
            def mm3(dst, a_hi, a_lo, b_hi, b_lo, start, stop):
                pe.matmul(dst, a_hi, b_hi, start=start, stop=False)
                pe.matmul(dst, a_lo, b_hi, start=False, stop=False)
                return pe.matmul(dst, a_hi, b_lo, start=False, stop=stop)

            def tile_piece(p, bank, x_hi=xt_hi, x_lo=xt_lo, cols=SEQ):
                s = p % 2
                wh, wl = (w[s][:, :].rearrange("p (k c) -> p k c", k=KT) for w in (w_hi, w_lo))
                for k in range(KT):
                    ins = mm3(ps[:, bank, 0:cols], wh[:, k, :], wl[:, k, :], x_hi[:, k, :], x_lo[:, k, :], k == 0, k == KT - 1)
                ins.then_inc(piece_done, 1)

            def natural(x, k, t):
                return x[:, k, t * P:(t + 1) * P]

            def residue(x, k, s):
                return x[:, k, s:s + 4 * (P - 1) + 1:4]

            def v_piece(p, k0, nk, cols, place, pick, x_hi=xt_hi, x_lo=xt_lo, tiles=TT):
                s = p % 2
                wh, wl = (w[s][:, 0:nk * cols].rearrange("p (k c) -> p k c", k=nk) for w in (w_hi, w_lo))
                for kk in range(nk):
                    k = k0 + kk
                    for t in range(tiles):
                        bank, c0, first, last = place(t)
                        ins = mm3(ps[:, bank, c0:c0 + cols], pick(x_hi, k, t), pick(x_lo, k, t), wh[:, kk, :], wl[:, kk, :],
                                  k == 0, k == KT - 1)
                ins.then_inc(piece_done, 1)

            def turn(src, t, bank):
                for hf in range(2):
                    for k in range(4):
                        ins = pe.transpose(ps[:, bank + hf, k * P:(k + 1) * P], src[:, t, (4 * hf + k) * P:(4 * hf + k + 1) * P],
                                           ident[:, :])
                    yield ins

            pe.wait_ge(const_ready, 5)
            for t in range(TT):
                pe.wait_ge(x_in[t], 16)
                for ins in turn(x_nat, t, 2 * t):
                    ins.then_inc(turned, 1)
            pe.wait_ge(small_in, 16 * 9)
            pe.wait_ge(turn_lo, 2 * TT)
            pe.transpose(ps[:, 6, 448:502], b_rows[:, :], ident[0:54, 0:54]).then_inc(seg_ps, 1)
            pe.matmul(ps[0:N_BIAS, 7, 0:SEG_CUT], rel[:, :], one_hot[:, 0:SEG_CUT], start=True, stop=True).then_inc(seg_ps, 1)
            pe.matmul(ps[0:N_BIAS, 6, 0:SEG_N - SEG_CUT], rel[:, :], one_hot[:, SEG_CUT:SEG_N], start=True,
                      stop=True).then_inc(seg_ps, 1)
            for p in range(PV0, PV12):
                pe.wait_ge(lo_done, p + 1)
                v_piece_two(pe, p, w_hi, w_lo, xt_hi, xt_lo, ps, 4 * p, TT, lambda t: (t // 2, 256 * (t % 2)), mm3, natural).then_inc(piece_done, 1)
            for p in range(PV12, PQA):
                pe.wait_ge(lo_done, p + 1)
                v_piece(p, 2 * (p - PV12), 2, 512, lambda t: (2 + t, 0, 0, 0), residue)
            for p in range(PQA, PVBC):
                n = p - PQA
                pe.wait_ge(lo_done, p + 1)
                if n == 0:
                    pe.wait_ge(seg_ready, 3)
                elif n == 2:
                    pe.wait_ge(proj_out, 2)
                elif n >= 4:
                    pe.wait_ge(proj_out, 6 + n - 3)
                tile_piece(p, (6, 7, 0, 1)[n % 4])
                if n == 3:
                    pe.wait_ge(mem_in, 16)
                    pe.wait_ge(proj_out, 6)
                    for m in range(2):
                        for ins in turn(mem_nat, m, 2 + 2 * m):
                            ins.then_inc(mem_turned, 1)

            def operands(kind, h, t):
                hf = slice(64 * (h % 2), 64 * (h % 2) + 64)
                rows = slice(t * P, (t + 1) * P)
                band = slice(max(t - 1, 0) * P, (t + 1) * P)
                if kind == "X":
                    return qx[hf, h // 2, rows], kx[hf, h // 2, :]
                if kind == "A0":
                    return qk[hf, T_QA + h // 2, rows], qk[hf, T_KA + h // 2, band]
                if kind in ("A1", "A2"):
                    g = 2 * int(kind[1])
                    return qk[hf, T_QA + g + h // 2, rows], qk[hf, T_KA + g + h // 2, rows]
                if kind == "B":
                    return qk[hf, T_QB + h // 2, rows], qk[hf, T_KB + h // 4, band]
                return qk[hf, T_QC + h // 2, rows], qk[hf, T_KC + h // 2, 0:(t + 1) * P]

            def scores(j):
                if 8 <= j < N_SELF:
                    if j == 8:
                        pe.wait_ge(neg_ready, units_before[8])
                    else:
                        pe.wait_ge(base_ready, TT * (j - 8))
                    pe.matmul(ps[:, 3, :], ident[0:N_CH, j - 8:j - 7].to_broadcast([N_CH, P]), ncum_t[:, :], start=True,
                              stop=True).then_inc(ncum_ps, 1)
                for b, units in enumerate(JOBS[j][0]):
                    bank = score_bank(j, b)
                    if j > 0:
                        prev = [(jj, bb) for jj, bb in bank_list if jj < j and score_bank(jj, bb) == bank]
                        if prev:
                            pe.wait_ge(neg_ready, bank_units_end[prev[-1]])
                    for kind, h, t, c0, cols, at in units:
                        q, k = operands(kind, h, t)
                        ins = pe.matmul(ps[:, bank, c0:c0 + cols], q, k, start=True, stop=True)
                    ins.then_inc(score_ps, 1)

            def v_tile(kind, h, kb):
                if kind == "A0":
                    return va[:, kb, h * DH:(h + 1) * DH]
                if kind in ("A1", "A2"):
                    g = int(kind[1])
                    return va[:, kb, 256 * g + h * DH:256 * g + (h + 1) * DH]
                if kind == "B":
                    return vbc[:, kb, (h // 4) * DH:(h // 4 + 1) * DH]
                if kind == "C":
                    return vbc[:, kb, 128 + h * DH:128 + (h + 1) * DH]
                return vx[:, kb, h * DH:(h + 1) * DH]

            def turn_probs(n):
                j, g = group_list[n]
                offs = JOBS[j][1][g][0]
                pe.wait_ge(prob_ready, units_before[j + 1])
                if n >= 2:
                    pe.wait_ge(pt_act if n % 2 == 0 else pt_dve, (n - 2) // 2 + 1)
                buf = probx if j >= N_SELF else prob
                for c, at in enumerate(offs):
                    ins = pe.transpose(ps[:, 4 + n % 2, c * P:(c + 1) * P], buf[:, SLOT(j), at:at + P], ident[:, :])
                ins.then_inc(pt_ps, 1)

            def times_v(n):
                j, g = group_list[n]
                _, products, kind, h, first, last = JOBS[j][1][g]
                m = acc_of[n]
                pe.wait_ge(pt_act if n % 2 == 0 else pt_dve, n // 2 + 1)
                if first and m >= 2:
                    if acc_kind[m - 2][0] == "X":
                        pe.wait_ge(oxl_done, m - 2 - (N_ACC - N_XH) + 1)
                    else:
                        pe.wait_ge(acc_dve if acc_by_dve[m - 2] else acc_act, acc_count[m - 2])
                hf = slice(64 * (h % 2), 64 * (h % 2) + 64)
                src = ptx if j >= N_SELF else pt
                for i, (kb, c0, cols, q0) in enumerate(products):
                    ins = pe.matmul(ps[hf, 6 + m % 2, q0:q0 + cols], v_tile(kind, h, kb), src[:, n % PT_SLOTS, c0:c0 + cols],
                                    start=(first and i == 0), stop=(last and i == len(products) - 1), skip_group_check=True)
                ins.then_inc(av_done, 1)

            def outputs(j):
                g0, g1 = groups_before[j], groups_before[j + 1]
                turn_probs(g0)
                for n in range(g0, g1):
                    if n + 1 < g1:
                        turn_probs(n + 1)
                    times_v(n)

            pe.wait_ge(proj_out, 18)
            for what, n in FRONT:
                if what == "scores":
                    scores(n)
                elif what == "piece":
                    p = n
                    pe.wait_ge(lo_done, p + 1)
                    if p < PQB:
                        v_piece(p, 2 * (p - PVBC), 2, VBC_N, lambda t: (4 + t, 0, 0, 0), natural)
                    else:
                        m = p - PQB
                        pe.wait_ge(proj_out, 22 if m < 4 else 22 + m - 3)
                        tile_piece(p, 4 + m % 4)
                elif what == "forward":
                    pe.wait_ge(neg_ready, units_before[4])
                    pe.wait_ge(parts_ready, 1)
                    pv = parts[:, :, :].rearrange("p c (t g x) -> p c t g x", t=TT, g=N_G)
                    for t in range(TT):
                        for g in range(2):
                            at = (t * 2 + g) * 24
                            for s in range(TT):
                                c = P * t - s + 3
                                ins = pe.matmul(ps[:, 0, at:at + 24], spread[:, c:c + P], pv[:, :, s, g + 1, :],
                                                start=(s == 0), stop=(s == TT - 1))
                    ins.then_inc(moved_ps, 1)
                    pe.wait_ge(lparts_ready, 1)
                    lv = lparts[:, :, :].rearrange("p c (t h) -> p c t h", t=TT)
                    for t in range(TT):
                        for s in range(t + 1):
                            m = upper[:, 0:P] if s == t else upper[:, P:2 * P]
                            ins = pe.matmul(ps[:, 1, 12 * t:12 * t + 12], m, lv[:, :, s, :], start=(s == 0), stop=(s == t))
                    ins.then_inc(cum_ps, 1)
                else:
                    pe.wait_ge(cum_ready, 1)
                    for t in range(TT):
                        ins = pe.transpose(ps[0:N_CH, 3, t * P:(t + 1) * P], cum[:, t, :], ident[:, :])
                    ins.then_inc(cumt_ps, 1)
                    pe.wait_ge(fparts_ready, 1)
                    fv = parts[:, :, 0:48].rearrange("p c (t g h) -> p c t g h", t=TT, g=N_G)
                    for g in range(2):
                        for s in range(TT):
                            at = (g * TT + s) * 12
                            for t in range(TT):
                                c = 384 + s - P * t
                                ins = pe.matmul(ps[:, 2, at:at + 12], shift[:, c:c + 4 * (P - 1) + 1:4], fv[:, :, t, g + 1, :],
                                                start=(t == 0), stop=(t == TT - 1))
                    ins.then_inc(back_ps, 1)
            pe.wait_ge(factor_ready, 2)
            pe.wait_ge(cumt_out, 1)
            pe.wait_ge(proj_out, 22 + 9)
            for what, n in BACKHALF:
                if what == "output":
                    outputs(n)
                else:
                    scores(n)

            pe.wait_ge(pt_act, (groups_before[N_SELF] + 1) // 2)
            pe.wait_ge(pt_dve, groups_before[N_SELF] // 2)
            pe.wait_ge(acc_act, c_act - N_XH)
            pe.wait_ge(acc_dve, N_AH)
            pe.wait_ge(neg_ready, units_before[N_SELF])
            pe.wait_ge(base_ready, TT * N_CH)
            with pe.Fori(0, N_PAIR) as i:
                for q in range(6):
                    p = PG + q
                    pe.wait_ge(lo_done, i * 8 + (p + 1))
                    if q == 0:
                        pe.wait_ge(merged_even, i)
                    if q == 1:
                        pe.wait_ge(merged_odd, i)
                    tile_piece(p, q)
                for b in range(2):
                    p = PG + 6 + b
                    pe.wait_ge(lo_done, i * 8 + (p + 1))
                    pe.wait_ge(o_lo_done, KT)
                    pe.wait_ge(sig_done, i * 6 + (1 if b == 0 else 4))
                    wh, wl = (w[p % 2][:, :].rearrange("p (k c) -> p k c", k=KT) for w in (w_hi, w_lo))
                    for bank, (k0, k1) in zip((6, 7, 0) if b == 0 else (1, 2, 3), ((0, 2), (2, 6), (6, 8))):
                        for k in range(k0, k1):
                            ins = mm3(ps[:, bank, :], wh[:, k, :], wl[:, k, :], o_hi[:, k, :], o_lo[:, k, :], k == k0, k == k1 - 1)
                    ins.then_inc(piece_done, 1)

            def rows_product(p0, n_k, a_hi, a_lo, ready, order):
                def part(p, k, t, start):
                    w_h, w_l = w_hi[p % 2], w_lo[p % 2]
                    for n in range(2):
                        cols = slice(n * 512, (n + 1) * 512)
                        ins = mm3(ps[:, 2 * t + n, :], a_hi[:, k, t * P:(t + 1) * P], a_lo[:, k, t * P:(t + 1) * P],
                                  w_h[:, cols], w_l[:, cols], start, k == n_k - 1)
                    return ins
                for k in range(n_k - 2):
                    pe.wait_ge(lo_done, p0 + k + 1)
                    ready(k)
                    for t in order:
                        if k == 0:
                            ready(-1 - t)
                        ins = part(p0 + k, k, t, k == 0)
                    ins.then_inc(piece_done, 1)
                pe.wait_ge(lo_done, p0 + n_k)
                ready(n_k - 2)
                ready(n_k - 1)
                for t in range(TT):
                    if n_k == 2:
                        ready(-1 - t)
                    ins = part(p0 + n_k - 2, n_k - 2, t, n_k == 2)
                    if t == TT - 1:
                        ins.then_inc(piece_done, 1)
                    ins = part(p0 + n_k - 1, n_k - 1, t, False)
                    ins.then_inc(piece_done if t == TT - 1 else rows_done, 1)

            def mix_ready(k):
                if k >= 0:
                    pe.wait_ge(merge_step, 6 * (k + 1))
                elif k == -1:
                    pe.wait_ge(merged_odd, N_PAIR)
            rows_product(PM, KT, m_hi, m_lo, mix_ready, MIX_ORDER)

            for n in range(2):
                pe.wait_ge(lo_done, PKX + n + 1)
                pe.wait_ge(mem_lo, 4)
                pe.wait_ge(y_done, 2)
                tile_piece(PKX + n, n, memt_hi, memt_lo, MEM)
            for n in range(2):
                pe.wait_ge(lo_done, PVX + n + 1)
                pe.wait_ge(y_done, 4)
                v_piece_two(pe, PVX + n, w_hi, w_lo, memt_hi, memt_lo, ps, 4 * n, 2, lambda t: (2, 256 * t), mm3, natural).then_inc(piece_done, 1)

            def norm_turn(first):
                for t in range(TT):
                    pe.wait_ge(gb_done, 2 * (first + t + 1))
                    pe.wait_ge(y_done, 2 * (first + t + 1))
                    for ins in turn(resid, t, 2 * t):
                        ins.then_inc(turned, 1)

            pe.wait_ge(memkv_out, 3)
            norm_turn(0)
            pe.wait_ge(turn_lo, 4 * TT)
            for n in range(2):
                pe.wait_ge(lo_done, PXQ + n + 1)
                tile_piece(PXQ + n, n)
            pe.wait_ge(xq_out, 2)
            for j in range(N_SELF, N_JOB):
                scores(j)
                if j >= N_SELF + 2:
                    outputs(j - 2)
            outputs(N_JOB - 2)
            outputs(N_JOB - 1)

            def xo_ready(k):
                if k == 0:
                    pe.wait_ge(oxl_done, N_XH)
                    pe.wait_ge(neg_ready, units_before[N_JOB])
            rows_product(PXO, 2, ox_hi, ox_lo, xo_ready, range(TT))
            norm_turn(TT)

            pe.wait_ge(turn_lo, 6 * TT)
            with pe.Fori(0, FF_PAIR) as i:
                for q in range(4):
                    p = PF + q
                    pe.wait_ge(lo_done, i * 4 + (p + 1))
                    if q == 0:
                        pe.wait_ge(silu_done, i * 2)
                    if q == 2:
                        pe.wait_ge(h_done, i * 2)
                    tile_piece(p, q)

            def out_ready(k):
                if k >= 0:
                    pe.wait_ge(h_done, k + 1)
                elif k == -1:
                    pe.wait_ge(h_done, FF_T - 1)
                elif k == -2:
                    pe.wait_ge(h_done, FF_T)
            rows_product(PO, FF_T, h_hi, h_lo, out_ready, MIX_ORDER)


def v_piece_two(pe, p, w_hi, w_lo, x_hi, x_lo, ps, k0, tiles, place, mm3, pick):
    wh, wl = (w[p % 2][:, :].rearrange("p (k c) -> p k c", k=4) for w in (w_hi, w_lo))
    for kk in range(4):
        k = k0 + kk
        for t in range(tiles):
            bank, c0 = place(t)
            a_hi, a_lo = pick(x_hi, k, t), pick(x_lo, k, t)
            dst = ps[:, bank, c0:c0 + 256]
            first = k == 0 and c0 == 0
            pe.matmul(dst, a_hi, wh[:, kk, :], start=first, stop=False, skip_group_check=True)
            pe.matmul(dst, a_lo, wh[:, kk, :], start=False, stop=False, skip_group_check=True)
            ins = pe.matmul(dst, a_hi, wl[:, kk, :], start=False, stop=(k == KT - 1), skip_group_check=True)
    return ins


_INS = ["x", "mem", "w_in", "b_in", "attn_sinks", "w_branch_a", "w_branch_b", "w_branch_c", "w_mix_out", "ln1_g", "ln1_b",
        "w_xq", "w_xkv", "w_xo", "ln2_g", "ln2_b", "w_ffn_in", "w_ffn_out", "ln3_g", "ln3_b", "rel_bias"]


def kernel(**inputs):
    import concourse.bacc as _bacc
    from concourse.bass_utils import run_bass_kernel_spmd as _run

    nc = _bacc.Bacc("TRN2", target_bir_lowering=False, num_devices=1)
    arrays = {f"in_{name}": np.ascontiguousarray(inputs[name]) for name in _INS}
    arrays["in_one_hot"], arrays["in_seg_mask"] = table_constants()
    aps = {name[3:]: nc.dram_tensor(name, a.shape, mybir.dt.from_np(a.dtype), kind="ExternalInput").ap()
           for name, a in arrays.items()}
    out = nc.dram_tensor("out", (1, SEQ, D), F32, kind="ExternalOutput").ap()
    build_layer(nc, aps, out)
    r = _run(nc, [arrays], core_ids=[0])
    return r.results[0]["out"]
```

```python
from contextlib import ExitStack

import numpy as np
import concourse.bass as bass
from concourse import mybir
from concourse.alu_op_type import AluOpType as ALU

F32 = mybir.dt.float32
F32R = mybir.dt.float32r
BF16 = mybir.dt.bfloat16
ACT = mybir.ActivationFunctionType

P = 128
D = 1024
SEQ = 512
MEM = 256
DH = 64
KT = D // P
TT = SEQ // P
N_AH, N_G = 4, 3
N_BH, N_BKV, N_CH, N_XH = 8, 2, 4, 4
D_FF = 2816
N_BIAS = N_G * N_AH + N_BH
N_BUCKETS, MAX_DIST = 32, 2048
ALPHA = 2.0 ** 0.25
LN_EPS = 1e-5
SCALE = DH ** -0.5
MASK = -1e30
HUGE = 3e38

QA, KA, VA0 = 0, 768, 1536
QB, KB, VB0 = 2304, 2816, 2944
QC, KC, VC0 = 3072, 3328, 3584
GATES = 3844
IN_W = GATES + 3 * D
VBC_N = 128 + 256 + 4

SEG1, SEG4, SEG16 = 3 * P - 1, 2 * P - 1, 2 * P - 1
SEG_N = SEG1 + SEG4 + SEG16
PT_SLOTS = 4
SEG_CUT = 448


def t5_bucket(dist):
    exact = N_BUCKETS // 2
    safe = np.maximum(dist, exact).astype(np.float32)
    large = exact + (np.log(safe / exact) / np.log(MAX_DIST / exact) * (N_BUCKETS - exact)).astype(np.int32)
    return np.where(dist < exact, dist, np.minimum(large, N_BUCKETS - 1)).astype(np.int32)


def table_constants():
    d1 = 2 * P - 1 - np.arange(SEG1)
    d4 = P - 1 - np.arange(SEG4)
    dist = np.concatenate([d1, 4 * d4, 4 * d4])
    bucket = t5_bucket(np.maximum(dist, 0))
    one_hot = (np.arange(N_BUCKETS)[:, None] == bucket[None]).astype(np.float32)
    a1 = np.where((d1 >= 0) & (d1 <= 128), 0.0, MASK)
    b1 = np.where((d1 >= 0) & (d1 <= 127), 0.0, MASK)
    a4 = np.where(d4 >= 0, 0.0, MASK)
    a16 = np.where((d4 >= 0) & (d4 % 4 == 0), 0.0, MASK)
    heads = [np.concatenate([b1 if h >= N_G * N_AH else a1, a4, a16]) for h in range(N_BIAS)]
    return one_hot, np.stack(heads).astype(np.float32)


T_QA, T_KA, T_QB, T_N = 0, 6, 18, 22
T_KB, T_KC, T_QC = T_KA, T_KA + 4, T_KA + 8
OUT_TILES = [0, 1, T_QB, T_QB + 1, T_QB + 2, T_QB + 3, T_QC, T_QC + 1]
N_OUT_AB = 5

PV0 = 0
PV12 = 2
PQA = 6
PVBC = 18
PQB = 22
PG = 31
PM = 63
PKX = 71
PVX = 73
PXQ = 75
PXO = 77
PF = 79
PO = PF + 2 * (D_FF // P)
P_END = PO + D_FF // P
N_PAIR = D // 256
FF_T = D_FF // P
FF_PAIR = FF_T // 2

FRONT = ([("piece", 18), ("scores", 0), ("piece", 19), ("scores", 1), ("piece", 20), ("scores", 2), ("piece", 21),
          ("scores", 3), ("piece", 22), ("piece", 23), ("piece", 24), ("forward", 0), ("piece", 25), ("piece", 26),
          ("piece", 27), ("back", 0), ("piece", 28), ("piece", 29), ("piece", 30)])
MIX_ORDER = [2, 3, 0, 1]
N_TAIL = 6


def band_at(t):
    return 0 if t == 0 else P + (t - 1) * 256


N_SELF = 12
N_GROUP_PAIRS = 22

C_AT = [0, 128, 384, 768]


def band_groups(base):
    own = [base + band_at(t) + (P if t else 0) for t in range(TT)]
    prev = [None] + [base + band_at(t) for t in range(1, TT)]
    return [([own[0], prev[1], own[1], prev[2]], [(0, 0, 256, 0), (1, 256, 256, 128)]),
            ([own[2], prev[3], own[3]], [(2, 0, 256, 256), (3, 256, 128, 384)])]


def make_jobs():
    jobs = []
    for h in range(N_AH):
        banks = [[("A0", h, 0, 0, 128, 0), ("A0", h, 1, 128, 256, 128)],
                 [("A0", h, 2, 0, 256, 384), ("A0", h, 3, 256, 256, 640)],
                 [("A1", h, s, s * P, P, 896 + s * P) for s in range(TT)],
                 [("A2", h, s, s * P, P, 1408 + s * P) for s in range(TT)]]
        g0 = band_groups(0)
        groups = [(g0[0][0], g0[0][1], "A0", h, True, False), (g0[1][0], g0[1][1], "A0", h, False, True)]
        for at, kind, base, first in ((1, "A1", 896, True), (3, "A2", 1408, False)):
            groups.insert(at, ([base + s * P for s in range(TT)], [(s, s * P, P, s * P) for s in range(TT)],
                               kind, h, first, not first))
        jobs.append((banks, groups))
    for pair in range(N_BH // 2):
        banks, groups = [], []
        for i in range(2):
            h, base = 2 * pair + i, 1024 * i
            banks += [[("B", h, 0, 0, 128, base), ("B", h, 1, 128, 256, base + 128)],
                      [("B", h, 2, 0, 256, base + 384), ("B", h, 3, 256, 256, base + 640)]]
            g = band_groups(base)
            for n in range(2):
                groups.insert(n * (i + 1) + i, (g[n][0], g[n][1], "B", h, n == 0, n == 1))
        jobs.append((banks, groups))
    for h in range(N_CH):
        banks = [[("C", h, 0, 0, 128, C_AT[0]), ("C", h, 2, 128, 384, C_AT[2])],
                 [("C", h, 1, 0, 256, C_AT[1])], [("C", h, 3, 0, 512, C_AT[3])]]
        groups = [([C_AT[t] for t in range(4)], [(0, 0, 512, 0)], "C", h, True, False),
                  ([C_AT[1] + P, C_AT[2] + P, C_AT[3] + P, C_AT[3] + 3 * P],
                   [(1, 0, 384, 128), (3, 384, 128, 384)], "C", h, False, False),
                  ([C_AT[2] + 2 * P, C_AT[3] + 2 * P], [(2, 0, 256, 256)], "C", h, False, True)]
        jobs.append((banks, groups))
    return jobs


def make_cross_jobs():
    jobs = []
    for half in range(2):
        banks = [[("X", h, 2 * half + i, 256 * i, 256, 512 * h + 256 * i) for i in range(2)] for h in range(N_XH)]
        groups = [([512 * h, 512 * h + 256, 512 * h + P, 512 * h + 256 + P], [(0, 0, 256, 0), (1, 256, 256, 0)],
                   "X", h, True, True) for h in range(N_XH)]
        jobs.append((banks, groups))
    return jobs


def front_for_splitters():
    order, split = [], PVBC
    for i, (what, n) in enumerate(FRONT):
        nxt = n if what == "piece" else min(m for w, m in FRONT[i:] if w == "piece")
        if what in ("scores", "piece") and nxt + 1 > split:
            split = nxt + 1
            order.append(("split", split))
        order.append((what, n))
    return order


def side_work(jobs):
    side = [[] for _ in range(N_GROUP_PAIRS)]
    for j in range(4, N_SELF):
        items = ([("base", j, 0)] if j >= 8 else []) + [("bank", j, b) for b in range(len(jobs[j][0]))]
        for i, item in enumerate(items):
            side[2 * j - 7 + i // 2].append(item)
    return side


def build_layer(nc, A, out):
    JOBS = make_jobs() + make_cross_jobs()
    SIDE = side_work(JOBS)
    N_JOB = len(JOBS)
    units_before, groups_before = [0], [0]
    for banks, groups in JOBS:
        units_before.append(units_before[-1] + sum(map(len, banks)))
        groups_before.append(groups_before[-1] + len(groups))
    bank_list = [(j, b) for j, (banks, _) in enumerate(JOBS) for b in range(len(banks))]
    bank_index = {jb: n for n, jb in enumerate(bank_list)}
    bank_units_end = {}
    n = 0
    for j, b in bank_list:
        n += len(JOBS[j][0][b])
        bank_units_end[(j, b)] = n
    group_list = []
    for j, (_, groups) in enumerate(JOBS):
        if groups[0][2] == "C":
            if j % 2 == 0:
                group_list += [(jj, g) for g in range(len(groups)) for jj in (j, j + 1)]
        else:
            group_list += [(j, g) for g in range(len(groups))]
    assert groups_before[N_SELF] == 2 * N_GROUP_PAIRS
    group_index = {jg: n for n, jg in enumerate(group_list)}
    acc_end, acc_of, acc_kind, acc_open = [], {}, [], {}
    for n, (j, g) in enumerate(group_list):
        kind, h, first, last = JOBS[j][1][g][2:]
        key = (j, "A12" if kind in ("A1", "A2") else kind, h)
        if first:
            acc_open[key] = len(acc_end)
            acc_end.append(None)
            acc_kind.append((kind, h, j))
        acc_of[n] = acc_open[key]
        if last:
            acc_end[acc_open[key]] = n
    N_ACC = len(acc_end)
    N_XACC = 2 * N_XH
    acc_by_dve = [m % 2 == 1 and k != "X" for m, (k, _, _) in enumerate(acc_kind)]
    acc_count = []
    c_act = c_dve = 0
    for by_dve in acc_by_dve:
        c_dve += by_dve
        c_act += not by_dve
        acc_count.append(c_dve if by_dve else c_act)
    accs_ended = {n: [m for m in range(N_ACC) if acc_end[m] in (n, n + 1)] for n in range(0, len(group_list), 2)}
    N_ACC_DVE = c_dve
    SLOT = lambda j: j % 4 if j < N_SELF else j - N_SELF

    w_in = A["w_in"][0].rearrange("(k p) n -> p k n", p=P)
    w_mix = A["w_mix_out"][0].rearrange("(k p) n -> p k n", p=P)
    w_br = [A[f"w_branch_{x}"][0].rearrange("(k p) n -> p k n", p=P) for x in "abc"]
    w_xkv = A["w_xkv"][0].rearrange("(k p) n -> p k n", p=P)
    w_xq = A["w_xq"][0].rearrange("(k p) n -> p k n", p=P)
    w_xo = A["w_xo"][0].rearrange("(k p) n -> p k n", p=P)
    w_f1 = A["w_ffn_in"][0].rearrange("(k p) n -> p k n", p=P)
    w_f2 = A["w_ffn_out"][0].rearrange("(k p) n -> p k n", p=P)
    rows1 = nc.dram_tensor("rows1", (N_AH + N_BH, P, SEG1), F32, kind="Internal")
    rows4 = nc.dram_tensor("rows4", (N_AH, P, SEG4), F32, kind="Internal")
    rows16 = nc.dram_tensor("rows16", (N_AH, P, SEG16), F32, kind="Internal")

    with ExitStack() as ctx:
        def sem(name):
            return ctx.enter_context(nc.semaphore(name))

        def sb(name, shape, dt=F32, stack=None):
            return (stack or ctx).enter_context(nc.sbuf_tensor(name, shape, dt))

        raw = [sb(f"raw{i}", [P, 2048]) for i in range(2)]
        w_hi = [sb(f"w_hi{i}", [P, 1024], F32R) for i in range(2)]
        w_lo = [sb(f"w_lo{i}", [P, 1024], F32R) for i in range(2)]
        xt_hi = sb("xt_hi", [P, KT, SEQ], F32R)
        xt_lo = sb("xt_lo", [P, KT, SEQ], F32R)
        ident = sb("ident", [P, P])
        shift = sb("shift", [P, 896], BF16)
        spread = sb("spread", [P, 516], BF16)
        upper = sb("upper", [P, 256], BF16)
        causal = sb("causal", [P, P])
        bias_t = sb("bias_t", [P, 54])
        sink = sb("sink", [P, N_BH])
        neg_sink = sb("neg_sink", [P, N_BH])
        stat_a = sb("stat_a", [P, TT, N_G, 2, N_AH])
        stat_nat = sb("stat_nat", [P, TT, N_G, 2, N_AH])
        comb_min = sb("comb_min", [P, TT, N_AH])
        comb_e = sb("comb_e", [P, TT, N_G, N_AH])
        comb_z = sb("comb_z", [P, TT, N_G, N_AH])
        factor = sb("factor", [P, TT, N_G, N_AH])
        factor_s = sb("factor_s", [P, 2, TT, N_AH])
        nmax = sb("nmax", [P, 64])
        psum_ = sb("psum_", [P, 64])
        rsum = sb("rsum", [P, 64])
        esink = sb("esink", [P, N_BH * TT])
        fl = sb("fl", [P, 3, TT, N_CH])
        logf = sb("logf", [P, TT, N_CH])
        lparts = sb("lparts", [P, 3, TT * N_CH], BF16)
        cum = sb("cum", [P, TT, N_CH])
        cum3 = sb("cum3", [P, TT, 3, N_CH])
        ncum_t = sb("ncum_t", [N_CH, SEQ])
        row_sum = sb("row_sum", [P, TT, 2])
        neg_mean = sb("neg_mean", [P, TT])
        sq_sum = sb("sq_sum", [P, TT])
        var = sb("var", [P, TT])
        rstd = sb("rstd", [P, TT])
        half = sb("half", [P, 1])

        with ExitStack() as st:
            memt_hi = sb("memt_hi", [P, KT, MEM], F32R, st)
            memt_lo = sb("memt_lo", [P, KT, MEM], F32R, st)
        sa = sb("sa", [P, 2, 512])
        ht = sb("ht", [P, 512])
        sb("hold_mem", [P, 2 * KT * MEM - 3 * 512])

        with ExitStack() as st:
            qk = sb("qk", [P, T_N, SEQ], F32, st)
            va = sb("va", [P, TT, 768], F32, st)
            vbc = sb("vbc", [P, TT, VBC_N], F32, st)
            tab1 = sb("tab1", [P, N_AH + N_BH, 256], F32, st)
            tab4 = sb("tab4", [P, N_AH, P], F32, st)
            tab16 = sb("tab16", [P, N_AH, P], F32, st)
            prob = sb("prob", [P, 4, 2048], F32, st)
            pt = sb("pt", [P, PT_SLOTS, 512], F32, st)
        with ExitStack() as st:
            sb("hold_qk", [P, T_N * SEQ + TT * 768 + TT * VBC_N], F32, st)
            mem_nat = sb("mem_nat", [P, 2, D], F32, st)
            sb("hold_tab", [P, (N_AH + N_BH) * 256 - 2 * D + 2 * N_AH * P], F32, st)
            x_nat = sb("x_nat", [P, TT, D], F32, st)
            one_hot = sb("one_hot", [N_BUCKETS, SEG_N], F32, st)
            seg_mask = sb("seg_mask", [N_BIAS, SEG_N], F32, st)
            seg_row = sb("seg_row", [N_BIAS, SEG_N], F32, st)
            b_rows = sb("b_rows", [54, P], F32, st)
            rel = sb("rel", [N_BUCKETS, N_BIAS], F32, st)
            sb("hold_p", [P, 4 * 2048 - TT * D - 3 * SEG_N - P - N_BIAS], F32, st)
            bv = sb("bv", [P, 768 + VBC_N], F32, st)
            parts = sb("parts", [P, 3, TT * N_G * 2 * N_AH], BF16, st)
            rest = sb("rest", [P, TT * N_G * 2 * N_AH], F32, st)
            moved = sb("moved", [P, TT * 2 * 24], F32, st)
        PAD_V = TT * (768 + VBC_N) - KT * SEQ
        with ExitStack() as keep:
            resid = sb("resid", [P, TT, D], F32, keep)
            gb = sb("gb", [P, 2, D], F32, keep)
            squares = sb("squares", [P, D], BF16, keep)
            with ExitStack() as st:
                sg = sb("sg", [P, 6, 512], F32, st)
                mt = sb("mt", [P, 3, 512], F32, st)
            with ExitStack() as st:
                k_hi = sb("k_hi", [P, 2, 1024], F32R, st)
                k_lo = sb("k_lo", [P, 2, 1024], F32R, st)
                sb("pad_k", [P, 512], F32, st)
                with ExitStack() as st2:
                    o_hi = sb("o_hi", [P, KT, SEQ], F32R, st2)
                    sb("pad_v", [P, PAD_V], F32, st2)
                    o_lo = sb("o_lo", [P, KT, SEQ], F32R, st2)
                    m_hi = sb("m_hi", [P, KT, SEQ], F32R, st2)
                    m_lo = sb("m_lo", [P, KT, SEQ], F32R, st2)
                with ExitStack() as st2:
                    x_hi = sb("x_hi", [P, 4, 1024], F32R, st2)
                    sb("pad_x", [P, PAD_V], F32, st2)
                    x_lo = sb("x_lo", [P, 4, 1024], F32R, st2)
                kx = sb("kx", [P, N_XH, MEM], F32, st)
                vx = sb("vx", [P, 2, N_XH * DH], F32, st)
                zero = sb("zero", [P, 256], F32, st)
                c_hi = sb("c_hi", [P, 3, 1024], F32R, st)
                c_lo = sb("c_lo", [P, 3, 1024], F32R, st)
                sb("pad_c", [P, 2 * KT * SEQ + PAD_V - N_XH * MEM - 2 * N_XH * DH - 256 - 6 * 1024], F32, st)
                qx = sb("qx", [P, 2, SEQ], F32, st)
                probx = sb("probx", [P, 2, 2048], F32, st)
                ptx = sb("ptx", [P, PT_SLOTS, 512], F32, st)
                ox_hi = sb("ox_hi", [P, 2, SEQ], F32R, st)
                ox_lo = sb("ox_lo", [P, 2, SEQ], F32R, st)
            with ExitStack() as st:
                h_hi = sb("h_hi", [P, FF_T, SEQ], F32R, st)
                h_lo = sb("h_lo", [P, FF_T, SEQ], F32R, st)

        ps = ctx.enter_context(nc.psum_tensor("ps", [P, 8, 512], F32))

        raw_in = [sem(f"raw_in{i}") for i in range(2)]
        hi_done, lo_done, piece_done = sem("hi_done"), sem("lo_done"), sem("piece_done")
        x_in = [sem(f"x_in{t}") for t in range(TT)]
        mem_in, small_in, resid_in = sem("mem_in"), sem("small_in"), sem("resid_in")
        const_ready = sem("const_ready")
        turned, turn_hi, turn_lo = sem("turned"), sem("turn_hi"), sem("turn_lo")
        mem_turned, mem_hi, mem_lo = sem("mem_turned"), sem("mem_hi"), sem("mem_lo")
        seg_ps, seg_ready, seg_out, table_in = sem("seg_ps"), sem("seg_ready"), sem("seg_out"), sem("table_in")
        proj_out = sem("proj_out")
        score_ps, ncum_ps, base_ready, diag_ready = sem("score_ps"), sem("ncum_ps"), sem("base_ready"), sem("diag_ready")
        neg_ready, exp_done, rsum_ready = sem("neg_ready"), sem("exp_done"), sem("rsum_ready")
        prob_dve, prob_pool = sem("prob_dve"), sem("prob_pool")
        esink_done = sem("esink_done")
        pt_ps, pt_act, pt_dve, av_done = sem("pt_ps"), sem("pt_act"), sem("pt_dve"), sem("av_done")
        acc_act, acc_dve = sem("acc_act"), sem("acc_dve")
        dve_step = sem("dve_step")
        pool_step = sem("pool_step")
        parts_ready, moved_ps, diff_ready, comb_exp = sem("parts_ready"), sem("moved_ps"), sem("diff_ready"), sem("comb_exp")
        fparts_ready, back_ps, factor_ready = sem("fparts_ready"), sem("back_ps"), sem("factor_ready")
        abs_ready, act_f, lparts_ready, cum_ps, cum_ready, cumt_ps, cumt_out = (
            sem("abs_ready"), sem("act_f"), sem("lparts_ready"), sem("cum_ps"), sem("cum_ready"), sem("cumt_ps"), sem("cumt_out"))
        o_hi_done, o_lo_done = sem("o_hi_done"), sem("o_lo_done")
        o_ab_hi, o_ab_lo = sem("o_ab_hi"), sem("o_ab_lo")
        sig_done, merged_even, merged_odd = sem("sig_done"), sem("merged_even"), sem("merged_odd")
        merge_step, ffn_step = sem("merge_step"), sem("ffn_step")
        rows_done, y_done, mean_done, sq_done, rstd_done, norm_done, gb_in = (
            sem("rows_done"), sem("y_done"), sem("mean_done"), sem("sq_done"), sem("rstd_done"), sem("norm_done"), sem("gb_in"))
        memkv_out, xq_ps, xq_out, zero_ready = sem("memkv_out"), sem("xq_ps"), sem("xq_out"), sem("zero_ready")
        oxl_done = sem("oxl_done")
        silu_done, h_done = sem("silu_done"), sem("h_done")
        stored = sem("stored")

        def stat_col(kind, h, t):
            if kind == "X":
                return 48 + 8 * (t // 2) + 2 * h + t % 2
            return {"B": 0, "C": 32}[kind] + h * TT + t

        POOL_SCALES = (1, 3, 5)

        def scale_units(j):
            for banks in JOBS[j][0]:
                for kind, h, t, _, cols, at in banks:
                    if kind == "A0":
                        f = factor[:, t, 0, h:h + 1]
                    elif kind in ("A1", "A2"):
                        f = factor_s[:, 0 if kind == "A1" else 1, t, h:h + 1]
                    else:
                        n = stat_col(kind, h, t)
                        f = rsum[:, n:n + 1]
                    yield (probx if kind == "X" else prob)[:, SLOT(j), at:at + cols], f

        def scaled_before(j):
            return sum(units_before[k + 1] - units_before[k] for k in range(j + 1) if (k in POOL_SCALES) == (j in POOL_SCALES))

        def scaled_for(j, g):
            read = (3, 8, 8, 12)[g] if j < N_AH else 2 * (g + 1) if j >= N_SELF else len(sum(JOBS[j][0], []))
            after = len(sum(JOBS[j][0], [])) - read
            return scaled_before(j) - after

        def score_bank(j, b):
            return b

        def acc_half(kind, h):
            i = (h + (kind in ("A1", "A2"))) % 2
            return slice(64 * i, 64 * i + 64)

        def pt_count(n):
            first_x = groups_before[N_SELF]
            if n >= first_x:
                return pt_act, (first_x + 1) // 2 + n - first_x + 1
            return (pt_act, pt_dve)[n % 2], n // 2 + 1

        def split_slot(p):
            for first, n, hi, lo in ((PM + 2, 4, x_hi, x_lo), (PKX, 2, k_hi, k_lo), (PXQ, 3, c_hi, c_lo), (PXO + 1, 1, k_hi, k_lo)):
                if first <= p < first + n:
                    return hi[:, p - first, :], lo[:, p - first, :]
            if PF + 2 <= p < PF + 4:
                return c_hi[:, PF + 3 - p, :], c_lo[:, PF + 3 - p, :]
            if PO + FF_T - N_TAIL <= p < PO + FF_T - 2:
                i = 2 * (p - (PO + FF_T - N_TAIL))
                return (x[:, i:i + 2, :].rearrange("p k c -> p (k c)") for x in (xt_hi, xt_lo))
            return w_hi[p % 2][:, :], w_lo[p % 2][:, :]

        def slot_spent(p):
            if PM + 2 <= p < PM + 6:
                return PM
            if PM + 6 <= p < PM + 8:
                return p - 5
            if PKX <= p < PVX:
                return PM
            if PVX <= p < PXQ:
                return p - 3
            if PXQ <= p < PXO + 1:
                return PM + 8
            if p == PXO + 1:
                return PKX + 1
            if PF <= p < PF + 2:
                return p - 5
            if PF + 2 <= p < PF + 4:
                return PXQ + 2
            if PO + FF_T - N_TAIL <= p < PO + FF_T - 2:
                return PO
            if PO + FF_T - 2 <= p:
                return p - 5
            return p - 1

        def raw_piece(p):
            hi, lo = split_slot(p)
            i, slot = piece_place(p)
            r = raw[slot]
            if p == PQB + 4:
                return r[:, 0:1024], hi[:, 0:1024], lo[:, 0:1024]
            if PVBC <= p < PQB:
                n = 2 * VBC_N
                return r[:, i * n:(i + 1) * n], hi[:, 0:n], lo[:, 0:n]
            if is_tile_piece(p):
                v = r[:, :].rearrange("p (k c) -> p k c", k=KT)[:, :, i * P:(i + 1) * P]
                return v, hi[:, :].rearrange("p (k c) -> p k c", k=KT), lo[:, :].rearrange("p (k c) -> p k c", k=KT)
            return r[:, i * 1024:(i + 1) * 1024], hi[:, :], lo[:, :]

        def is_tile_piece(p):
            return PQA <= p < PVBC or PQB <= p < PM or PKX <= p < PVX or PXQ <= p < PXO or PF <= p < PO

        def chunk_of(p):
            return p // 2 if p < PQB + 4 else (PQB + 4) // 2 if p == PQB + 4 else (p + 1) // 2

        def piece_place(p):
            c = chunk_of(p)
            first = 2 * c if p <= PQB + 4 else 2 * c - 1
            return p - first, c % 2

        def last_piece(c):
            return 2 * c + 1 if c < 13 else 2 * c

        def chunk_loads(c):
            r = raw[c % 2]
            k8 = r[:, :].rearrange("p (k c) -> p k c", k=KT)
            p = last_piece(c)
            if c == 0:
                return [(k8, w_in[:, :, VA0:VA0 + 256])]
            if p < PQA:
                k0 = 4 * (c - 1)
                return [(r[:, :].rearrange("p (k c) -> p k c", k=4), w_in[:, k0:k0 + 4, VA0 + 256:VA0 + 768])]
            if p < PVBC:
                n0 = 256 * (c - 3)
                return [(k8, w_in[:, :, n0:n0 + 256])]
            if p < PQB:
                k0 = 4 * (c - 9)
                v = r[:, 0:4 * VBC_N].rearrange("p (k c) -> p k c", k=4)
                return [(v[:, :, 0:128], w_in[:, k0:k0 + 4, VB0:VB0 + 128]),
                        (v[:, :, 128:VBC_N], w_in[:, k0:k0 + 4, VC0:VC0 + 260])]
            if c < 13:
                n0 = QB + 256 * (c - 11)
                return [(k8, w_in[:, :, n0:n0 + 256])]
            if c == 13:
                return [(r[:, 0:1024].rearrange("p (k c) -> p k c", k=KT), w_in[:, :, KB:KB + 128])]
            if c < 16:
                n0 = QC + 256 * (c - 14)
                return [(k8, w_in[:, :, n0:n0 + 256])]
            if PM <= p < PKX:
                k0 = 2 * (c - 32)
                return [(r[:, :].rearrange("p (k c) -> p k c", k=2), w_mix[:, k0:k0 + 2, :])]
            if p < PVX:
                return [(k8, w_xkv[:, :, 0:256])]
            if p < PXQ:
                return [(k8, w_xkv[:, :, 256:512])]
            if p < PXO:
                return [(k8, w_xq[:, :, :])]
            return [(r[:, :].rearrange("p (k c) -> p k c", k=2), w_xo[:, :, :])]

        CG, CM, CF, CO = 16, 32, 40, 40 + 2 * FF_PAIR
        arrivals = [0, 0]
        arrive_at = {}
        for c in range(CO + FF_PAIR):
            n_dma = 6 // 2 if CG <= c < CM and (c - CG) % 4 == 3 else len(chunk_loads(c)) if c < CG or CM <= c < CF else 1
            arrivals[c % 2] += 16 * n_dma
            arrive_at[c] = arrivals[c % 2]
        G_ARR = [32, 64]

        block = ctx.enter_context(nc.Block())

        @block.sync
        def _(sp):
            for t in range(3):
                sp.dma_start(x_nat[:, t, :], A["x"][0, t * P:(t + 1) * P, :]).then_inc(x_in[t], 16)
            sp.dma_start(raw[0][:, :].rearrange("p (k c) -> p k c", k=KT), chunk_loads(0)[0][1]).then_inc(raw_in[0], 16)
            for t in range(3, TT):
                sp.dma_start(x_nat[:, t, :], A["x"][0, t * P:(t + 1) * P, :]).then_inc(x_in[t], 16)

            def load(c):
                if c >= 2:
                    sp.wait_ge(lo_done, last_piece(c - 2) + 1)
                for dst, src in chunk_loads(c):
                    sp.dma_start(dst, src).then_inc(raw_in[c % 2], 16)

            load(1)
            for dst, src in ((b_rows[0:30, :], A["b_in"][0:1, 0:30 * P].rearrange("a (n p) -> (a n) p", p=P)),
                             (b_rows[30:54, :], A["b_in"][0:1, GATES:IN_W].rearrange("a (n p) -> (a n) p", p=P)),
                             (rel[:, :], A["rel_bias"]), (one_hot[:, :], A["one_hot"]), (seg_mask[:, :], A["seg_mask"]),
                             (bv[:, 0:768], A["b_in"][0:1, VA0:VA0 + 768].to_broadcast([P, 768])),
                             (bv[:, 768:896], A["b_in"][0:1, VB0:VB0 + 128].to_broadcast([P, 128])),
                             (bv[:, 896:1156], A["b_in"][0:1, VC0:VC0 + 260].to_broadcast([P, 260])),
                             (sink[:, :], A["attn_sinks"][0:1, :].to_broadcast([P, N_BH]))):
                sp.dma_start(dst, src).then_inc(small_in, 16)
            for c in range(2, CG):
                load(c)
                if c == 3:
                    sp.dma_start(mem_nat[:, :, :], A["mem"][0].rearrange("(m p) n -> p m n", p=P)).then_inc(mem_in, 16)
            for i in range(N_PAIR):
                for q in range(4):
                    sp.wait_ge(lo_done, i * 8 + (PG + 2 * q - 2))
                    k8 = raw[q % 2][:, :].rearrange("p (k c) -> p k c", k=KT)
                    if q < 3:
                        n0 = GATES + q * D + i * 256
                        sp.dma_start(k8, w_in[:, :, n0:n0 + 256]).then_inc(raw_in[q % 2], 16)
                    else:
                        for w, (k0, k1) in zip(w_br, ((0, 2), (2, 6), (6, 8))):
                            sp.dma_start(k8[:, k0:k1, :], w[:, :, i * 256:(i + 1) * 256]).then_inc(raw_in[1], 16)
            for c in range(CM, CF):
                load(c)
                if c == CM:
                    sp.wait_ge(o_ab_lo, N_OUT_AB)
                    sp.wait_ge(o_lo_done, KT - N_OUT_AB)
                    sp.dma_start(resid[:, :, :], A["x"][0].rearrange("(t p) n -> p t n", p=P)).then_inc(resid_in, 16)
                    for i, w in enumerate(("ln1_g", "ln1_b")):
                        sp.dma_start(gb[:, i, :], A[w][0:1, :].to_broadcast([P, D])).then_inc(gb_in, 16)
            sp.wait_ge(norm_done, TT)
            for i, w in enumerate(("ln2_g", "ln2_b")):
                sp.dma_start(gb[:, i, :], A[w][0:1, :].to_broadcast([P, D])).then_inc(gb_in, 16)
            for i in range(FF_PAIR):
                for q in range(2):
                    sp.wait_ge(lo_done, i * 4 + (PF + 2 * q - 2))
                    n0 = i * 256 + q * D_FF
                    sp.dma_start(raw[q][:, :].rearrange("p (k c) -> p k c", k=KT),
                                 w_f1[:, :, n0:n0 + 256]).then_inc(raw_in[q], 16)
            sp.wait_ge(norm_done, 2 * TT)
            for i, w in enumerate(("ln3_g", "ln3_b")):
                sp.dma_start(gb[:, i, :], A[w][0:1, :].to_broadcast([P, D])).then_inc(gb_in, 16)
            for n in range(FF_PAIR):
                sp.wait_ge(lo_done, PO + 2 * n - 2)
                sp.dma_start(raw[n % 2][:, :].rearrange("p (k c) -> p k c", k=2),
                             w_f2[:, 2 * n:2 * n + 2, :]).then_inc(raw_in[n % 2], 16)
            for t in range(TT - 1):
                sp.wait_ge(norm_done, 2 * TT + t + 1)
                sp.dma_start(out[0, t * P:(t + 1) * P, :], resid[:, t, :]).then_inc(stored, 16)
            for c in range(2):
                sp.wait_ge(norm_done, 3 * TT + c)
                cols = slice(512 * c, 512 * c + 512)
                sp.dma_start(out[0, (TT - 1) * P:, cols], resid[:, TT - 1, cols]).then_inc(stored, 16)
            sp.wait_ge(stored, 16 * (TT + 1))

        @block.gpsimd
        def _(pool):
            pool.memset(ident[:, :], 0.0).then_inc(pool_step, 1)
            pool.wait_ge(pool_step, 1)
            pool.affine_select(out=ident[:, :], in_=ident[:, :], compare_op=ALU.not_equal, fill=1.0, base=0,
                               pattern=[[-1, P]], channel_multiplier=1).then_inc(const_ready, 1)
            steps = 1
            for m, v in ((shift, 0.0), (spread, 0.0), (upper, 1.0), (causal, 0.0), (half, -0.5)):
                pool.memset(m[:, :], v).then_inc(pool_step, 1)
                steps += 1
            pool.wait_ge(pool_step, steps)
            pool.affine_select(out=shift[:, :], in_=shift[:, :], compare_op=ALU.not_equal, fill=1.0, base=384,
                               pattern=[[-1, 896]], channel_multiplier=1).then_inc(const_ready, 1)
            pool.affine_select(out=spread[:, :], in_=spread[:, :], compare_op=ALU.not_equal, fill=1.0, base=3,
                               pattern=[[-1, 516]], channel_multiplier=4).then_inc(const_ready, 1)
            pool.affine_select(out=upper[:, 0:P], in_=upper[:, 0:P], compare_op=ALU.is_ge, fill=0.0, base=0,
                               pattern=[[1, P]], channel_multiplier=-1).then_inc(const_ready, 1)
            pool.affine_select(out=causal[:, :], in_=causal[:, :], compare_op=ALU.is_ge, fill=MASK, base=0,
                               pattern=[[-1, P]], channel_multiplier=1).then_inc(const_ready, 1)
            pool.wait_ge(const_ready, 5)
            for hf in range(2):
                pool.memset(qk[64 - 64 * hf:128 - 64 * hf, T_KA + hf:T_KA + 12:2, :], 0.0).then_inc(zero_ready, 1)
            pool.wait_ge(seg_ready, 3)
            copies = ((rows1, 0, 0, N_AH, 0, SEG1), (rows1, N_AH, N_G * N_AH, N_BH, 0, SEG1),
                      (rows4, 0, N_AH, N_AH, SEG1, SEG4), (rows16, 0, 2 * N_AH, N_AH, SEG1 + SEG4, SEG16))
            for rows, to, h0, nh, at, width in copies:
                pool.dma_start(rows.ap()[to:to + nh, :, :],
                               seg_row[h0:h0 + nh, at:at + width].unsqueeze(1).broadcast_to([nh, P, width])).then_inc(seg_out, 16)
            pool.wait_ge(seg_out, 16 * len(copies))
            pool.wait_ge(mem_turned, 4)
            for tab, rows, nh, width, cols in ((tab1, rows1, N_AH + N_BH, SEG1, 256), (tab4, rows4, N_AH, SEG4, P),
                                               (tab16, rows16, N_AH, SEG16, P)):
                for h in range(nh):
                    pool.dma_start(tab[:, h, :], bass.AP(rows, h * P * width + P - 1, [[width - 1, P], [1, cols]])).then_inc(table_in, 16)

            def scale_probs(j):
                for v, f in scale_units(j):
                    pool.tensor_scalar(v, v, f, None, ALU.mult).then_inc(prob_pool, 1)

            def mask_diagonals(j):
                for kind, h, t, _, cols, at in sorted(sum(JOBS[j][0], []), key=lambda u: u[2]):
                    pool.wait_ge(base_ready, TT * (j - 8) + t + 1)
                    v = prob[:, SLOT(j), at + cols - P:at + cols]
                    pool.tensor_tensor(v, v, causal[:, :], ALU.add).then_inc(diag_ready, 1)

            pool.wait_ge(factor_ready, 2)
            for j in POOL_SCALES:
                if j >= N_AH:
                    pool.wait_ge(rsum_ready, j - N_AH + 1)
                scale_probs(j)
            for j, split_now in zip(range(8, N_SELF), ((0,), (1,), (2,), (3, 4))):
                mask_diagonals(j)
                if j == 8:
                    pool.wait_ge(av_done, groups_before[N_AH])
                    pool.wait_ge(neg_ready, units_before[8])
                    pool.wait_ge(acc_dve, N_AH)
                for m in split_now:
                    if m >= 2:
                        pool.wait_ge(acc_act, m + 3)
                        pool.wait_ge(acc_dve, m + 3)
                    pool.tensor_copy(o_hi[:, m, :], qk[:, OUT_TILES[m], :]).then_inc(o_ab_hi, 1)
                    pool.wait_ge(o_ab_hi, m + 1)
                    pool.tensor_tensor(o_lo[:, m, :], qk[:, OUT_TILES[m], :], o_hi[:, m, :].bitcast(F32),
                                       ALU.subtract).then_inc(o_ab_lo, 1)
            for n in range(3 * TT):
                t = n % TT
                pool.wait_ge(sq_done, n + 1)
                pool.tensor_scalar(var[:, t:t + 1], sq_sum[:, t:t + 1], 1.0 / D, LN_EPS, ALU.mult, ALU.add).then_inc(pool_step, 1)
                steps += 1
                pool.wait_ge(pool_step, steps)
                pool.tensor_tensor(rstd[:, t:t + 1], var[:, t:t + 1], half[:, 0:1], ALU.pow).then_inc(rstd_done, 1)

        @block.scalar
        def _(act):
            def split(p):
                c = chunk_of(p)
                act.wait_ge(raw_in[c % 2], arrive_at[c])
                if p >= 2:
                    act.wait_ge(piece_done, slot_spent(p))
                src, hi, _ = raw_piece(p)
                act.copy(hi, src).then_inc(hi_done, 1)

            def turn_drain(n, count):
                t, hf = n // 2, n % 2
                act.wait_ge(turned, count + 1)
                act.copy(xt_hi[:, 4 * hf:4 * hf + 4, t * P:(t + 1) * P],
                         ps[:, 2 * t + hf, :].rearrange("p (k c) -> p k c", k=4)).then_inc(turn_hi, 1)

            def exps(j, b):
                units = JOBS[j][0][b]
                first = bank_units_end[(j, b)] - len(units)
                for u, (kind, h, t, _, cols, at) in enumerate(units):
                    buf = probx if kind == "X" else prob
                    if kind[0] == "A":
                        g = int(kind[1])
                        nm, dn = stat_a[:, t, g, 0, h:h + 1], stat_a[:, t, g, 1, h:h + 1]
                    else:
                        c = stat_col(kind, h, t)
                        nm, dn = nmax[:, c:c + 1], psum_[:, c:c + 1]
                    act.wait_ge(neg_ready, first + u + 1)
                    v = buf[:, SLOT(j), at:at + cols]
                    act.activation(v, v, ACT.Exp, bias=nm, scale=-1.0, accum_out=dn).then_inc(exp_done, 1)
                if kind == "B" and b % 2 == 1:
                    act.activation(esink[:, h * TT:(h + 1) * TT], nmax[:, h * TT:(h + 1) * TT], ACT.Exp,
                                   bias=sink[:, h:h + 1]).then_inc(esink_done, 1)

            def fox_base(j):
                h = j - 8
                act.wait_ge(ncum_ps, h + 1)
                for t in range(TT):
                    n = (t + 1) * P
                    act.activation(prob[:, SLOT(j), C_AT[t]:C_AT[t] + n], ps[:, 3, 0:n], ACT.Identity,
                                   bias=cum[:, t, h:h + 1]).then_inc(base_ready, 1)

            def pt_drain(n):
                if pt_count(n)[0] is pt_act:
                    j, g = group_list[n]
                    act.wait_ge(pt_ps, n + 1)
                    if n >= PT_SLOTS:
                        act.wait_ge(av_done, n - PT_SLOTS + 1)
                    w = P * len(JOBS[j][1][g][0])
                    dst = ptx if j >= N_SELF else pt
                    act.copy(dst[:, n % PT_SLOTS, 0:w], ps[:, 4 + n % 2, 0:w]).then_inc(pt_act, 1)

            def acc_drain(m):
                kind, h, j = acc_kind[m]
                half_ = slice(64 * (h % 2), 64 * (h % 2) + 64)
                if acc_by_dve[m]:
                    return
                act.wait_ge(av_done, acc_end[m] + 1)
                src = ps[half_, 6 + m % 2, :]
                if kind == "X":
                    q0 = 256 * (j - N_SELF)
                    act.copy(ox_hi[half_, h // 2, q0:q0 + 256], src[:, 0:256]).then_inc(acc_act, 1)
                    return
                tile = {"A0": 0, "B": T_QB, "C": T_QC}[kind] + h // 2
                act.copy(qk[half_, tile, :], src).then_inc(acc_act, 1)

            act.wait_ge(const_ready, 1)
            act.copy(esink[:, 0:1], ident[:, 0:1])
            for n in range(2 * TT):
                turn_drain(n, n)
                if n == 3:
                    split(0)
            for p in range(0, 18):
                split(p + 1)
                if p == PQA + 3:
                    for n in range(4):
                        act.wait_ge(mem_turned, n + 1)
                        m, hf = n // 2, n % 2
                        act.copy(memt_hi[:, 4 * hf:4 * hf + 4, m * P:(m + 1) * P],
                                 ps[:, 2 + n, :].rearrange("p (k c) -> p k c", k=4)).then_inc(mem_hi, 1)
            for what, n in front_for_splitters():
                if what == "split":
                    split(n)
                elif what == "scores":
                    for b in range(len(JOBS[n][0])):
                        exps(n, b)
                elif what == "piece":
                    if n == 22:
                        act.wait_ge(abs_ready, 1)
                        act.activation(fl[:, 1, :, :], fl[:, 0, :, :], ACT.Exp).then_inc(act_f, 1)
                        act.wait_ge(act_f, 1)
                        act.activation(fl[:, 2, :, :], fl[:, 1, :, :], ACT.Ln, bias=1.0).then_inc(act_f, 1)
                elif what == "forward":
                    act.wait_ge(diff_ready, 1)
                    act.activation(comb_e[:, :, :, :], comb_e[:, :, :, :], ACT.Exp).then_inc(comb_exp, 1)
            def out_hi(m):
                act.copy(o_hi[:, m, :], qk[:, OUT_TILES[m], :]).then_inc(o_hi_done, 1)

            pt_drain(0)
            for i in range(N_GROUP_PAIRS + 1):
                for m in accs_ended[2 * i - 2] if i else []:
                    acc_drain(m)
                if i == N_GROUP_PAIRS:
                    break
                if i + 1 < N_GROUP_PAIRS:
                    pt_drain(2 * i + 2)
                if i == 0:
                    split(PG + 1)
                for what, j, b in SIDE[i]:
                    if what == "base":
                        fox_base(j)
                for what, j, b in SIDE[i - 1] if i else []:
                    if what == "bank":
                        exps(j, b)
            act.wait_ge(av_done, groups_before[N_SELF])
            act.wait_ge(acc_act, c_act - N_XACC)
            act.wait_ge(acc_dve, N_ACC_DVE)
            for m in range(N_OUT_AB, KT):
                out_hi(m)
            act.wait_ge(o_ab_lo, N_OUT_AB)
            act.wait_ge(o_lo_done, KT - N_OUT_AB)

            def gate_iteration(i, last, first=False):
                for q in range(8):
                    p = PG + q
                    np_, wrap = (p + 1, 0) if q < 7 else (PG, 1)
                    if last and q == 7:
                        split(PM)
                    elif not (first and q == 0):
                        gate_split(i, np_ - PG, wrap)
                    if q < 6:
                        br, b = q // 2, q % 2
                        act.wait_ge(piece_done, i * 8 + (p + 1))
                        act.activation(sg[:, q, :], ps[:, q, :], ACT.Sigmoid,
                                       bias=bias_t[:, bass.ds(i * 2 + (30 + 8 * br + b), 1)]).then_inc(sig_done, 1)

            def gate_split(i, q, wrap):
                p = PG + q
                c = q // 2
                slot = c % 2
                base = arrive_at[CG - 2 + slot]
                within = {0: 16, 1: 16, 2: 32, 3: 64}[c]
                act.wait_ge(raw_in[slot], (i + wrap) * G_ARR[slot] + (base + within))
                act.wait_ge(piece_done, (i + wrap) * 8 + (p - 1))
                v = raw[slot][:, :].rearrange("p (k c) -> p k c", k=KT)[:, :, (q % 2) * P:(q % 2 + 1) * P]
                act.copy(w_hi[p % 2][:, :].rearrange("p (k c) -> p k c", k=KT), v).then_inc(hi_done, 1)

            gate_iteration(0, False, first=True)
            with act.Fori(1, N_PAIR - 1) as i:
                gate_iteration(i, False)
            gate_iteration(N_PAIR - 1, True)
            for p in range(PM + 1, PM + 8):
                split(p)
            act.wait_ge(merge_step, 2 * N_PAIR * 6)
            split(PKX)
            split(PKX + 1)

            def square(n):
                t = n % TT
                act.wait_ge(mean_done, n + 1)
                if n:
                    act.wait_ge(sq_done, n)
                act.activation(squares[:, :], resid[:, t, :], ACT.Square, bias=neg_mean[:, t:t + 1],
                               accum_out=sq_sum[:, t:t + 1]).then_inc(sq_done, 1)

            def turn_tile(k, t):
                for hf in range(2):
                    turn_drain(2 * t + hf, 2 * TT * k + 2 * t + hf)

            square(0)
            square(1)
            turn_tile(1, 0)
            square(2)
            turn_tile(1, 1)
            square(3)
            turn_tile(1, 2)
            for p in range(PVX, PXO + 2):
                split(p)
            turn_tile(1, 3)
            for h in range(N_XH):
                exps(N_SELF, h)
            split(PF)
            gx = groups_before[N_SELF]
            for h in range(N_XH):
                exps(N_SELF + 1, h)
                if h == 0:
                    split(PF + 1)
                if h >= 1:
                    pt_drain(gx + h - 1)
            for n in range(gx, groups_before[N_JOB] + 1, 2):
                for m in accs_ended[n - 2] if n > gx else []:
                    acc_drain(m)
                for nn in (n + 2, n + 3):
                    if gx + 3 <= nn < groups_before[N_JOB]:
                        pt_drain(nn)
            square(TT)
            square(TT + 1)
            turn_tile(2, 0)
            turn_tile(2, 1)
            square(TT + 2)
            split(PF + 2)
            split(PF + 3)
            square(TT + 3)
            turn_tile(2, 2)
            turn_tile(2, 3)

            F_BASE = [arrive_at[CF - 2], arrive_at[CF - 1]]

            def ffn_split(i, q, wrap):
                p = PF + q
                slot = (q // 2) % 2
                act.wait_ge(raw_in[slot], (i + wrap) * 16 + (F_BASE[slot] + 16))
                act.wait_ge(piece_done, (i + wrap) * 4 + (p - 1))
                v = raw[slot][:, :].rearrange("p (k c) -> p k c", k=KT)[:, :, (q % 2) * P:(q % 2 + 1) * P]
                act.copy(w_hi[p % 2][:, :].rearrange("p (k c) -> p k c", k=KT), v).then_inc(hi_done, 1)

            def ffn_iteration(i, first=False, last=False):
                for q in range(4):
                    if last and q == 3:
                        split(PO)
                    elif not (first and q < 3):
                        ffn_split(i, (q + 1) % 4, (q + 1) // 4)
                    if q < 2:
                        act.wait_ge(piece_done, i * 4 + (PF + q + 1))
                        if not first:
                            act.wait_ge(h_done, i * 2)
                        act.activation(sa[:, q, :], ps[:, q, :], ACT.Silu).then_inc(silu_done, 1)

            ffn_iteration(0, first=True)
            with act.Fori(1, FF_PAIR - 1) as i:
                ffn_iteration(i)
            ffn_iteration(FF_PAIR - 1, last=True)
            for n in range(1, FF_T):
                split(PO + n)
            for t in range(TT):
                square(2 * TT + t)

        @block.vector
        def _(dve):
            chain = [0]

            def link(ins):
                chain[0] += 1
                ins.then_inc(dve_step, 1)
                dve.wait_ge(dve_step, chain[0])

            def f32(ap):
                return ap.bitcast(F32)

            def rest_of(p):
                dve.wait_ge(hi_done, p + 1)
                src, hi, lo = raw_piece(p)
                dve.tensor_tensor(lo, src, f32(hi), ALU.subtract).then_inc(lo_done, 1)

            def turn_drain(n, count):
                t, hf = n // 2, n % 2
                dve.wait_ge(turn_hi, count + 1)
                at = (slice(None), slice(4 * hf, 4 * hf + 4), slice(t * P, (t + 1) * P))
                dve.tensor_tensor(xt_lo[at], ps[:, 2 * t + hf, :].rearrange("p (k c) -> p k c", k=4),
                                  f32(xt_hi[at]), ALU.subtract).then_inc(turn_lo, 1)

            def split3(dst, src, tmp):
                link(dve.tensor_copy(dst[:, 0, :], src))
                link(dve.tensor_tensor(tmp, src, dst[:, 0, :], ALU.subtract))
                link(dve.tensor_copy(dst[:, 1, :], tmp))
                link(dve.tensor_tensor(tmp, tmp, dst[:, 1, :], ALU.subtract))
                return dve.tensor_copy(dst[:, 2, :], tmp)

            def strided(bank):
                return ps[:, bank, :].rearrange("p (i s) -> p s i", s=4)

            def drain_piece(p):
                if p == PV0 + 1:
                    dve.wait_ge(piece_done, p + 1)
                    for b in range(2):
                        dve.tensor_tensor(va[:, 2 * b:2 * b + 2, 0:256], ps[:, b, :].rearrange("p (t c) -> p t c", t=2),
                                          bv[:, 0:256].unsqueeze(1).broadcast_to([P, 2, 256]), ALU.add).then_inc(proj_out, 1)
                elif p == PV12 + 3:
                    dve.wait_ge(piece_done, p + 1)
                    for t in range(TT):
                        dve.tensor_tensor(va[:, t, 256:768], ps[:, 2 + t, :], bv[:, 256:768], ALU.add).then_inc(proj_out, 1)
                elif PQA <= p < PVBC:
                    n = p - PQA
                    dve.wait_ge(piece_done, p + 1)
                    bank = (6, 7, 0, 1)[n % 4]
                    if n < 6:
                        if n % 6 < 2:
                            dst, src = qk[:, n, :], ps[:, bank, :]
                        else:
                            dst, src = qk[:, n, :].rearrange("p (s i) -> p s i", s=4), strided(bank)
                        dve.tensor_scalar(dst, src, bias_t[:, n:n + 1], SCALE, ALU.add, ALU.mult).then_inc(proj_out, 1)
                    else:
                        for hf in range(2):
                            half_ = slice(64 * hf, 64 * hf + 64)
                            dst, src = qk[half_, T_KA + 2 * (n - 6) + hf, :], ps[half_, bank, :]
                            if n % 6 >= 2:
                                dst, src = dst.rearrange("p (s i) -> p s i", s=4), src.rearrange("p (i s) -> p s i", s=4)
                            ins = dve.tensor_scalar(dst, src, bias_t[half_, n:n + 1], None, ALU.add)
                        ins.then_inc(proj_out, 1)
                elif p == PVBC + 3:
                    dve.wait_ge(piece_done, p + 1)
                    for t in range(TT):
                        dve.tensor_tensor(vbc[:, t, :], ps[:, 4 + t, 0:VBC_N], bv[:, 768:768 + VBC_N], ALU.add).then_inc(proj_out, 1)
                    dve.wait_ge(proj_out, 18 + 4)
                    dve.scalar_tensor_tensor(out=fl[:, 0, :, :], in0=vbc[:, :, 384:388], scalar=-1.0,
                                             in1=vbc[:, :, 384:388], op0=ALU.mult, op1=ALU.min).then_inc(abs_ready, 1)
                elif PQB <= p < PG:
                    n = p - PQB
                    dve.wait_ge(piece_done, p + 1)
                    bank = 4 + (n + 3) % 4
                    if n == 4:
                        dve.wait_ge(score_ps, bank_index[(N_AH - 1, 3)] + 1)
                        for kv in range(2):
                            for hf in range(2):
                                ins = dve.tensor_scalar(qk[64 * hf:64 * hf + 64, T_KB + 2 * kv + hf, :], ps[64 * kv:64 * kv + 64, bank, :],
                                                        bias_t[64 * kv:64 * kv + 64, 22:23], None, ALU.add)
                        ins.then_inc(proj_out, 1)
                    elif n < 7:
                        tile, col = (T_QB + n, 18 + n) if n < 4 else (T_QC + n - 5, 24 + n - 5)
                        dve.tensor_scalar(qk[:, tile, :], ps[:, bank, :], bias_t[:, col:col + 1], SCALE,
                                          ALU.add, ALU.mult).then_inc(proj_out, 1)
                    else:
                        for hf in range(2):
                            half_ = slice(64 * hf, 64 * hf + 64)
                            ins = dve.tensor_scalar(qk[half_, T_KC + 2 * (n - 7) + hf, :], ps[half_, bank, :],
                                                    bias_t[half_, 26 + n - 7:27 + n - 7], None, ALU.add)
                        ins.then_inc(proj_out, 1)

            def scores_out(j, banks=None):
                for b in banks or range(len(JOBS[j][0])):
                    units = JOBS[j][0][b]
                    dve.wait_ge(score_ps, bank_index[(j, b)] + 1)
                    bank = score_bank(j, b)
                    for kind, h, t, c0, cols, at in units:
                        buf = probx if kind == "X" else prob
                        dst = buf[:, SLOT(j), at:at + cols]
                        start = HUGE
                        if kind == "A0":
                            bias, nm = tab1[:, h, 256 - cols:256], stat_a[:, t, 0, 0, h:h + 1]
                        elif kind == "A1":
                            bias, nm = tab4[:, h, :], stat_a[:, t, 1, 0, h:h + 1]
                        elif kind == "A2":
                            bias, nm = tab16[:, h, :], stat_a[:, t, 2, 0, h:h + 1]
                        else:
                            c = stat_col(kind, h, t)
                            nm = nmax[:, c:c + 1]
                            if kind == "B":
                                bias, start = tab1[:, N_AH + h, 256 - cols:256], neg_sink[:, h:h + 1]
                            elif kind == "C":
                                dve.wait_ge(diag_ready, TT * h + t + 1)
                                bias = dst
                            else:
                                bias = zero[:, 0:cols]
                        dve.tensor_tensor_reduce(dst, ps[:, bank, c0:c0 + cols], bias, -1.0, start, ALU.add, ALU.min,
                                                 nm).then_inc(neg_ready, 1)

            def sums_out(j):
                if j < N_AH:
                    return
                kind = JOBS[j][1][0][2]
                h0 = JOBS[j][1][0][3]
                nh = 2 if kind == "B" else 1
                c = stat_col(kind, h0, 0)
                v = slice(c, c + nh * TT)
                dve.wait_ge(exp_done, units_before[j + 1])
                if kind == "B":
                    dve.wait_ge(esink_done, h0 + 2)
                    link(dve.tensor_tensor(psum_[:, v], psum_[:, v], esink[:, v], ALU.add))
                dve.reciprocal(rsum[:, v], psum_[:, v]).then_inc(rsum_ready, 1)
                dve.wait_ge(rsum_ready, j - N_AH + 1)

            def scale_probs(j, part=slice(0, None)):
                for v, f in list(scale_units(j))[part]:
                    dve.tensor_scalar(v, v, f, None, ALU.mult).then_inc(prob_dve, 1)

            def pt_drain(n):
                if pt_count(n)[0] is pt_dve:
                    j, g = group_list[n]
                    dve.wait_ge(pt_ps, n + 1)
                    if n >= PT_SLOTS:
                        dve.wait_ge(av_done, n - PT_SLOTS + 1)
                    w = P * len(JOBS[j][1][g][0])
                    dst = ptx if j >= N_SELF else pt
                    dve.tensor_copy(dst[:, n % PT_SLOTS, 0:w], ps[:, 4 + n % 2, 0:w]).then_inc(pt_dve, 1)

            def acc_drain(m):
                kind, h, j = acc_kind[m]
                half_ = slice(64 * (h % 2), 64 * (h % 2) + 64)
                if kind == "X":
                    dve.wait_ge(acc_act, acc_count[m])
                    q0 = 256 * (j - N_SELF)
                    cols = slice(q0, q0 + 256)
                    dve.tensor_tensor(ox_lo[half_, h // 2, cols], ps[half_, 6 + m % 2, 0:256], f32(ox_hi[half_, h // 2, cols]),
                                      ALU.subtract).then_inc(oxl_done, 1)
                elif acc_by_dve[m] and kind != "A1":
                    dve.wait_ge(av_done, acc_end[m] + 1)
                    tile = {"B": T_QB, "C": T_QC}[kind] + h // 2
                    dve.tensor_copy(qk[half_, tile, :], ps[half_, 6 + m % 2, :]).then_inc(acc_dve, 1)
                elif acc_by_dve[m]:
                    dve.wait_ge(av_done, acc_end[m] + 1)
                    dve.wait_ge(acc_act, acc_count[m - 1])
                    o = qk[half_, h // 2, :].rearrange("p (i s) -> p i s", s=4)
                    dve.tensor_tensor(o, ps[acc_half(kind, h), 6 + m % 2, :].rearrange("p (s i) -> p i s", s=4), o,
                                      ALU.add).then_inc(acc_dve, 1)

            for n in range(2 * TT):
                turn_drain(n, n)
                if n == 3:
                    rest_of(0)
            def small_tables():
                dve.wait_ge(seg_ps, 3)
                dve.tensor_copy(bias_t[:, :], ps[:, 6, 448:502]).then_inc(seg_ready, 1)
                dve.tensor_tensor(seg_row[:, 0:SEG_CUT], ps[0:N_BIAS, 7, 0:SEG_CUT], seg_mask[:, 0:SEG_CUT], ALU.add).then_inc(seg_ready, 1)
                dve.tensor_tensor(seg_row[:, SEG_CUT:SEG_N], ps[0:N_BIAS, 6, 0:SEG_N - SEG_CUT], seg_mask[:, SEG_CUT:SEG_N],
                                  ALU.add).then_inc(seg_ready, 1)
                link(dve.tensor_scalar(neg_sink[:, :], sink[:, :], -1.0, None, ALU.mult))
                dve.wait_ge(seg_ready, 1)

            dve.wait_ge(small_in, 16 * 9)
            for p in range(0, 18):
                rest_of(p + 1)
                drain_piece(p)
                if p == PV12 - 1:
                    small_tables()
                if p == PQA + 3:
                    for n in range(4):
                        m, hf = n // 2, n % 2
                        dve.wait_ge(mem_hi, n + 1)
                        at = (slice(None), slice(4 * hf, 4 * hf + 4), slice(m * P, (m + 1) * P))
                        dve.tensor_tensor(memt_lo[at], ps[:, 2 + n, :].rearrange("p (k c) -> p k c", k=4),
                                          f32(memt_hi[at]), ALU.subtract).then_inc(mem_lo, 1)
            dve.wait_ge(table_in, 16 * (N_AH + N_BH + 2 * N_AH))
            for what, n in front_for_splitters():
                if what == "split":
                    rest_of(n)
                elif what == "scores":
                    scores_out(n)
                elif what == "piece":
                    drain_piece(n)
                    if n == 28:
                        dve.wait_ge(factor_ready, 2)
                        scale_probs(0)
                    if n == 23:
                        dve.wait_ge(act_f, 2)
                        dve.scalar_tensor_tensor(out=logf[:, :, :], in0=vbc[:, :, 384:388], scalar=0.0, in1=fl[:, 2, :, :],
                                                 op0=ALU.min, op1=ALU.subtract).then_inc(dve_step, 1)
                        chain[0] += 1
                        dve.wait_ge(dve_step, chain[0])
                        split3(lparts, logf[:, :, :].rearrange("p t h -> p (t h)"),
                               fl[:, 0, :, :].rearrange("p t h -> p (t h)")).then_inc(lparts_ready, 1)
                    if n == 23:
                        dve.wait_ge(exp_done, units_before[N_AH])
                        split3(parts, stat_a[:, :, :, :, :].rearrange("p t g d h -> p (t g d h)"), rest[:, :]).then_inc(parts_ready, 1)
                elif what == "forward":
                    dve.wait_ge(cum_ps, 1)
                    link(dve.tensor_copy(cum3[:, :, :, :].rearrange("p t c h -> p (t c h)"), ps[:, 1, 0:48]))
                    link(dve.tensor_tensor(cum[:, :, :], cum3[:, :, 0, :], cum3[:, :, 1, :], ALU.add))
                    dve.tensor_tensor(cum[:, :, :], cum[:, :, :], cum3[:, :, 2, :], ALU.add).then_inc(cum_ready, 1)
                    dve.wait_ge(moved_ps, 1)
                    link(dve.tensor_copy(moved[:, :], ps[:, 0, 0:192]))
                    mvw = moved[:, :].rearrange("p (t g c x) -> p t g c x", t=TT, g=2, c=3)
                    nat = stat_nat[:, :, :, :, :].rearrange("p t g d h -> p t g (d h)")
                    link(dve.tensor_copy(nat[:, :, 0, :], stat_a[:, :, 0, :, :].rearrange("p t d h -> p t (d h)")))
                    link(dve.tensor_tensor(nat[:, :, 1:3, :], mvw[:, :, :, 0, :], mvw[:, :, :, 1, :], ALU.add))
                    link(dve.tensor_tensor(nat[:, :, 1:3, :], nat[:, :, 1:3, :], mvw[:, :, :, 2, :], ALU.add))
                    nm = [stat_nat[:, :, g, 0, :] for g in range(3)]
                    link(dve.tensor_tensor(comb_min[:, :, :], nm[0], nm[1], ALU.min))
                    link(dve.tensor_tensor(comb_min[:, :, :], comb_min[:, :, :], nm[2], ALU.min))
                    dve.tensor_tensor(comb_e[:, :, :, :], comb_min[:, :, :].unsqueeze(2).broadcast_to([P, TT, N_G, N_AH]),
                                      stat_nat[:, :, :, 0, :], ALU.subtract).then_inc(diff_ready, 1)
                    dve.wait_ge(comb_exp, 1)
                    link(dve.tensor_tensor(comb_z[:, :, :, :], comb_e[:, :, :, :], stat_nat[:, :, :, 1, :], ALU.mult))
                    link(dve.tensor_tensor(comb_min[:, :, :], comb_z[:, :, 0, :], comb_z[:, :, 1, :], ALU.add))
                    link(dve.tensor_tensor(comb_min[:, :, :], comb_min[:, :, :], comb_z[:, :, 2, :], ALU.add))
                    link(dve.reciprocal(comb_min[:, :, :], comb_min[:, :, :]))
                    link(dve.tensor_tensor(factor[:, :, :, :], comb_e[:, :, :, :],
                                           comb_min[:, :, :].unsqueeze(2).broadcast_to([P, TT, N_G, N_AH]), ALU.mult))
                    dve.wait_ge(moved_ps, 1)
                    split3(parts[:, :, 0:48], factor[:, :, :, :].rearrange("p t g h -> p (t g h)"),
                           rest[:, 0:48]).then_inc(fparts_ready, 1)
                elif what == "back":
                    dve.wait_ge(cumt_ps, 1)
                    dve.tensor_scalar(ncum_t[:, :], ps[0:N_CH, 3, :], -1.0, None, ALU.mult).then_inc(cumt_out, 1)
                    dve.wait_ge(back_ps, 1)
                    link(dve.tensor_copy(moved[:, 0:96], ps[:, 2, 0:96]))
                    msw = moved[:, 0:96].rearrange("p (g s c h) -> p g s c h", g=2, s=TT, c=3)
                    for g in range(2):
                        link(dve.tensor_tensor(factor_s[:, g, :, :], msw[:, g, :, 0, :], msw[:, g, :, 1, :], ALU.add))
                        dve.tensor_tensor(factor_s[:, g, :, :], factor_s[:, g, :, :], msw[:, g, :, 2, :], ALU.add).then_inc(factor_ready, 1)
            def out_lo(m):
                dve.wait_ge(o_hi_done, m - N_OUT_AB + 1)
                dve.tensor_tensor(o_lo[:, m, :], qk[:, OUT_TILES[m], :], f32(o_hi[:, m, :]), ALU.subtract).then_inc(o_lo_done, 1)

            pt_drain(1)
            for i in range(N_GROUP_PAIRS + 1):
                for m in accs_ended[2 * i - 2] if i else []:
                    acc_drain(m)
                if i == N_GROUP_PAIRS:
                    break
                if i + 1 < N_GROUP_PAIRS:
                    pt_drain(2 * i + 3)
                if i == 0:
                    rest_of(PG + 1)
                if i < 2:
                    scale_probs(2, slice(6 * i, 6 * i + 6))
                j = i // 2 + 2
                if N_AH <= j < N_SELF - 1:
                    if i % 2 == 0:
                        sums_out(j)
                    if j not in POOL_SCALES:
                        scale_probs(j, slice(4 * (i % 2), 4 * (i % 2) + 4))
                for what, jj, b in SIDE[i]:
                    if what == "bank":
                        scores_out(jj, [b])
                if i == 2 * N_SELF - 7:
                    sums_out(N_SELF - 1)
                    scale_probs(N_SELF - 1)
            for m in range(N_OUT_AB, KT):
                out_lo(m)

            def gate_rest(i, q, wrap):
                p = PG + q
                slot = (q // 2) % 2
                dve.wait_ge(hi_done, (i + wrap) * 8 + (p + 1))
                v = raw[slot][:, :].rearrange("p (k c) -> p k c", k=KT)[:, :, (q % 2) * P:(q % 2 + 1) * P]
                s = p % 2
                dve.tensor_tensor(w_lo[s][:, :].rearrange("p (k c) -> p k c", k=KT), v,
                                  f32(w_hi[s][:, :]).rearrange("p (k c) -> p k c", k=KT), ALU.subtract).then_inc(lo_done, 1)

            MERGE_STEPS = 6

            def gate_iteration(i, last):
                for q in range(8):
                    if 0 < q < 7:
                        gate_rest(i, q + 1, 0)
                    if q >= 6:
                        b = q - 6
                        dve.wait_ge(piece_done, i * 8 + (PG + q + 1))
                        dve.wait_ge(sig_done, i * 6 + 6)
                        banks = (6, 7, 0) if b == 0 else (1, 2, 3)
                        at = bass.ds(i * 1024 + b * 512, 512)
                        mh = m_hi[:, :, :].rearrange("p k c -> p (k c)")[:, at]
                        ml = m_lo[:, :, :].rearrange("p k c -> p (k c)")[:, at]
                        step = lambda n: i * (2 * MERGE_STEPS) + (b * MERGE_STEPS + n)
                        if not (isinstance(i, int) and step(0) == 0):
                            dve.wait_ge(merge_step, step(0))
                        dve.tensor_tensor(mt[:, 0, :], ps[:, banks[0], :], sg[:, b, :], ALU.mult).then_inc(merge_step, 1)
                        dve.tensor_tensor(mt[:, 1, :], ps[:, banks[1], :], sg[:, 2 + b, :], ALU.mult).then_inc(merge_step, 1)
                        if last:
                            rest_of(PM + b)
                        else:
                            gate_rest(i, b, 1)
                        dve.tensor_tensor(mt[:, 2, :], ps[:, banks[2], :], sg[:, 4 + b, :], ALU.mult).then_inc(
                            merged_even if b == 0 else merged_odd, 1)
                        dve.wait_ge(merge_step, step(2))
                        dve.tensor_tensor(mt[:, 0, :], mt[:, 0, :], mt[:, 1, :], ALU.add).then_inc(merge_step, 1)
                        dve.wait_ge(merge_step, step(3))
                        dve.wait_ge(merged_even if b == 0 else merged_odd, i + 1)
                        dve.tensor_tensor(mt[:, 0, :], mt[:, 0, :], mt[:, 2, :], ALU.add).then_inc(merge_step, 1)
                        dve.wait_ge(merge_step, step(4))
                        dve.tensor_copy(mh, mt[:, 0, :]).then_inc(merge_step, 1)
                        dve.wait_ge(merge_step, step(5))
                        dve.tensor_tensor(ml, mt[:, 0, :], f32(mh), ALU.subtract).then_inc(merge_step, 1)

            gate_iteration(0, False)
            with dve.Fori(1, N_PAIR - 1) as i:
                gate_iteration(i, False)
            gate_iteration(N_PAIR - 1, True)

            def norm_sums(n):
                t = n % TT
                if n == 0:
                    dve.wait_ge(resid_in, 16)
                for c in range(2):
                    if (t, c) == (TT - 1, 1):
                        dve.wait_ge(piece_done, (PM + KT, PXO + 2, P_END)[n // TT])
                    else:
                        dve.wait_ge(rows_done, (2 * TT - 1) * (n // TT) + 2 * t + c + 1)
                    v = resid[:, t, c * 512:(c + 1) * 512]
                    dve.scalar_tensor_tensor(out=v, in0=v, scalar=ALPHA, in1=ps[:, 2 * t + c, :], op0=ALU.mult, op1=ALU.add,
                                             accum_out=row_sum[:, t, c:c + 1]).then_inc(y_done, 1)
                dve.wait_ge(y_done, 2 * n + 2)
                dve.tensor_scalar(neg_mean[:, t:t + 1], row_sum[:, t, 0:1], row_sum[:, t, 1:2], -1.0 / D, ALU.add,
                                  ALU.mult).then_inc(mean_done, 1)

            def norm_last(n):
                t = n % TT
                link(dve.scalar_tensor_tensor(out=sa[:, :, :].rearrange("p a c -> p (a c)"), in0=resid[:, t, :],
                                              scalar=neg_mean[:, t:t + 1], in1=gb[:, 0, :], op0=ALU.add, op1=ALU.mult))
                dve.wait_ge(sq_done, n + 1)
                dve.wait_ge(rstd_done, n + 1)
                for c in range(2):
                    cols = slice(512 * c, 512 * c + 512)
                    dve.scalar_tensor_tensor(out=resid[:, t, cols], in0=sa[:, c, :], scalar=rstd[:, t:t + 1], in1=gb[:, 1, cols],
                                             op0=ALU.mult, op1=ALU.add).then_inc(norm_done, 1)

            def norm_out(n):
                t = n % TT
                v = resid[:, t, :]
                if t == 0:
                    dve.wait_ge(gb_in, 32 * (n // TT + 1))
                dve.wait_ge(sq_done, n + 1)
                link(dve.scalar_tensor_tensor(out=v, in0=v, scalar=neg_mean[:, t:t + 1], in1=gb[:, 0, :], op0=ALU.add, op1=ALU.mult))
                dve.wait_ge(rstd_done, n + 1)
                dve.scalar_tensor_tensor(out=v, in0=v, scalar=rstd[:, t:t + 1], in1=gb[:, 1, :], op0=ALU.mult,
                                         op1=ALU.add).then_inc(norm_done, 1)

            def turn_tile(k, t):
                for hf in range(2):
                    turn_drain(2 * t + hf, 2 * TT * k + 2 * t + hf)

            for p in range(PM + 2, PKX + 2):
                rest_of(p)
            norm_sums(0)
            norm_out(0)
            norm_sums(1)
            norm_out(1)
            turn_tile(1, 0)
            norm_sums(2)
            norm_out(2)
            turn_tile(1, 1)
            norm_sums(3)
            norm_out(3)
            rest_of(PVX)
            turn_tile(1, 2)
            rest_of(PVX + 1)
            dve.memset(zero[:, :], 0.0).then_inc(zero_ready, 1)
            for hf in range(2):
                dve.memset(kx[64 - 64 * hf:128 - 64 * hf, hf:N_XH:2, :], 0.0).then_inc(zero_ready, 1)
            for n in range(2):
                dve.wait_ge(piece_done, PKX + n + 1)
                for hf in range(2):
                    half_ = slice(64 * hf, 64 * hf + 64)
                    ins = dve.tensor_copy(kx[half_, 2 * n + hf, :], ps[half_, n, 0:MEM])
                ins.then_inc(memkv_out, 1)
                rest_of(PXQ + n)
            dve.wait_ge(piece_done, PVX + 2)
            dve.tensor_copy(vx[:, :, :], ps[:, 2, :].rearrange("p (m c) -> p m c", m=2)).then_inc(memkv_out, 1)
            rest_of(PXO)
            rest_of(PXO + 1)

            def queries_out(half_t):
                for n in range(2):
                    if half_t == 0:
                        dve.wait_ge(xq_ps, n + 1)
                    else:
                        dve.wait_ge(piece_done, PXQ + n + 1)
                    dve.tensor_scalar(qx[:, n, 256 * half_t:256 * half_t + 256], ps[:, 4 + 2 * half_t + n, 0:256], SCALE, None,
                                      ALU.mult).then_inc(xq_out, 1)

            def head_scaled(j, h):
                c = stat_col("X", h, 2 * (j - N_SELF))
                dve.wait_ge(exp_done, units_before[j] + 2 * (h + 1))
                dve.reciprocal(rsum[:, c:c + 2], psum_[:, c:c + 2]).then_inc(rsum_ready, 1)
                dve.wait_ge(rsum_ready, N_SELF - N_AH + N_XH * (j - N_SELF) + h + 1)
                scale_probs(j, slice(2 * h, 2 * h + 2))

            queries_out(0)
            turn_tile(1, 3)
            dve.wait_ge(zero_ready, 5)
            for h in range(N_XH):
                scores_out(N_SELF, [h])
                if h >= 2:
                    head_scaled(N_SELF, h - 2)
            head_scaled(N_SELF, 2)
            head_scaled(N_SELF, 3)
            queries_out(1)
            rest_of(PF)
            for h in range(N_XH):
                scores_out(N_SELF + 1, [h])
                if h >= 2:
                    head_scaled(N_SELF + 1, h - 2)
            head_scaled(N_SELF + 1, 2)
            head_scaled(N_SELF + 1, 3)
            x_accs = range(N_ACC - N_XACC, N_ACC)
            for m in x_accs[0:6]:
                acc_drain(m)
                if m == x_accs[1]:
                    rest_of(PF + 1)
            norm_sums(TT)
            acc_drain(x_accs[6])
            acc_drain(x_accs[7])
            norm_sums(TT + 1)
            norm_out(TT)
            norm_out(TT + 1)
            turn_tile(2, 0)
            norm_sums(TT + 2)
            turn_tile(2, 1)
            norm_sums(TT + 3)
            rest_of(PF + 2)
            norm_out(TT + 2)
            norm_out(TT + 3)
            rest_of(PF + 3)
            turn_tile(2, 2)
            turn_tile(2, 3)

            def ffn_rest(i, q, wrap):
                p = PF + q
                slot, s = (q // 2) % 2, p % 2
                dve.wait_ge(hi_done, (i + wrap) * 4 + (p + 1))
                v = raw[slot][:, :].rearrange("p (k c) -> p k c", k=KT)[:, :, (q % 2) * P:(q % 2 + 1) * P]
                dve.tensor_tensor(w_lo[s][:, :].rearrange("p (k c) -> p k c", k=KT), v,
                                  f32(w_hi[s][:, :]).rearrange("p (k c) -> p k c", k=KT), ALU.subtract).then_inc(lo_done, 1)

            def ffn_iteration(i, first=False, last=False):
                for q in range(4):
                    if last and q == 3:
                        rest_of(PO)
                    elif not (first and q < 3):
                        ffn_rest(i, (q + 1) % 4, (q + 1) // 4)
                    if q >= 2:
                        b = q - 2
                        dve.wait_ge(piece_done, i * 4 + (PF + q + 1))
                        dve.wait_ge(silu_done, i * 2 + (b + 1))
                        at = bass.ds(i * 1024 + b * 512, 512)
                        hh = h_hi[:, :, :].rearrange("p k c -> p (k c)")[:, at]
                        hl = h_lo[:, :, :].rearrange("p k c -> p (k c)")[:, at]
                        if not (first and b == 0):
                            dve.wait_ge(ffn_step, i * 4 + 2 * b)
                            dve.wait_ge(h_done, i * 2 + b)
                        dve.tensor_tensor(ht[:, :], ps[:, 2 + b, :], sa[:, b, :], ALU.mult).then_inc(ffn_step, 1)
                        dve.wait_ge(ffn_step, i * 4 + (2 * b + 1))
                        dve.tensor_copy(hh, ht[:, :]).then_inc(ffn_step, 1)
                        dve.wait_ge(ffn_step, i * 4 + (2 * b + 2))
                        dve.tensor_tensor(hl, ht[:, :], f32(hh), ALU.subtract).then_inc(h_done, 1)

            ffn_iteration(0, first=True)
            with dve.Fori(1, FF_PAIR - 1) as i:
                ffn_iteration(i)
            ffn_iteration(FF_PAIR - 1, last=True)
            for n in range(1, FF_T):
                rest_of(PO + n)
            for t in range(TT):
                norm_sums(2 * TT + t)
                if t < TT - 1:
                    norm_out(2 * TT + t)
                else:
                    dve.wait_ge(mean_done, 3 * TT)
                    norm_last(2 * TT + t)

        @block.tensor
        def _(pe):
            def mm3(dst, a_hi, a_lo, b_hi, b_lo, start, stop):
                pe.matmul(dst, a_hi, b_hi, start=start, stop=False)
                pe.matmul(dst, a_lo, b_hi, start=False, stop=False)
                return pe.matmul(dst, a_hi, b_lo, start=False, stop=stop)

            def tile_piece(p, bank, a_hi=xt_hi, a_lo=xt_lo, cols=slice(0, SEQ), at=0, signal=True):
                wh, wl = (w.rearrange("p (k c) -> p k c", k=KT) for w in split_slot(p))
                n = cols.stop - cols.start
                for k in range(KT):
                    ins = mm3(ps[:, bank, at:at + n], wh[:, k, :], wl[:, k, :], a_hi[:, k, cols], a_lo[:, k, cols],
                              k == 0, k == KT - 1)
                if signal:
                    ins.then_inc(piece_done, 1)
                return ins

            def natural(x, k, t):
                return x[:, k, t * P:(t + 1) * P]

            def residue(x, k, s):
                return x[:, k, s:s + 4 * (P - 1) + 1:4]

            def v_piece(p, k0, nk, cols, place, pick, x_hi=xt_hi, x_lo=xt_lo, tiles=TT):
                s = p % 2
                wh, wl = (w[s][:, 0:nk * cols].rearrange("p (k c) -> p k c", k=nk) for w in (w_hi, w_lo))
                for kk in range(nk):
                    k = k0 + kk
                    for t in range(tiles):
                        bank, c0, first, last = place(t)
                        ins = mm3(ps[:, bank, c0:c0 + cols], pick(x_hi, k, t), pick(x_lo, k, t), wh[:, kk, :], wl[:, kk, :],
                                  k == 0, k == KT - 1)
                ins.then_inc(piece_done, 1)

            def turn(src, t, bank):
                for hf in range(2):
                    for k in range(4):
                        ins = pe.transpose(ps[:, bank + hf, k * P:(k + 1) * P], src[:, t, (4 * hf + k) * P:(4 * hf + k + 1) * P],
                                           ident[:, :])
                    yield ins

            pe.wait_ge(const_ready, 1)

            def piece_zero(pair):
                return v_piece_two(pe, 0, w_hi, w_lo, xt_hi, xt_lo, ps, 0, pair, lambda t: (t // 2, 256 * (t % 2)), mm3, natural)

            for t in range(TT):
                pe.wait_ge(x_in[t], 16)
                for ins in turn(x_nat, t, 2 * t):
                    ins.then_inc(turned, 1)
            pe.wait_ge(turn_lo, 4)
            pe.wait_ge(lo_done, 1)
            piece_zero((0, 1))
            pe.wait_ge(turn_lo, 2 * TT)
            piece_zero((2, 3)).then_inc(piece_done, 1)
            for p in range(PV0 + 1, PV12):
                pe.wait_ge(lo_done, p + 1)
                v_piece_two(pe, p, w_hi, w_lo, xt_hi, xt_lo, ps, 4 * p, range(TT), lambda t: (t // 2, 256 * (t % 2)), mm3, natural).then_inc(piece_done, 1)
            pe.wait_ge(small_in, 16 * 9)
            pe.transpose(ps[:, 6, 448:502], b_rows[:, :], ident[0:54, 0:54]).then_inc(seg_ps, 1)
            pe.matmul(ps[0:N_BIAS, 7, 0:SEG_CUT], rel[:, :], one_hot[:, 0:SEG_CUT], start=True, stop=True).then_inc(seg_ps, 1)
            pe.matmul(ps[0:N_BIAS, 6, 0:SEG_N - SEG_CUT], rel[:, :], one_hot[:, SEG_CUT:SEG_N], start=True,
                      stop=True).then_inc(seg_ps, 1)
            for p in range(PV12, PQA):
                pe.wait_ge(lo_done, p + 1)
                v_piece(p, 2 * (p - PV12), 2, 512, lambda t: (2 + t, 0, 0, 0), residue)
            for p in range(PQA, PVBC):
                n = p - PQA
                pe.wait_ge(lo_done, p + 1)
                if n == 0:
                    pe.wait_ge(seg_ready, 3)
                elif n == 2:
                    pe.wait_ge(proj_out, 2)
                elif n >= 4:
                    pe.wait_ge(proj_out, 6 + n - 3)
                tile_piece(p, (6, 7, 0, 1)[n % 4])
                if n == 3:
                    pe.wait_ge(mem_in, 16)
                    pe.wait_ge(proj_out, 6)
                    for m in range(2):
                        for ins in turn(mem_nat, m, 2 + 2 * m):
                            ins.then_inc(mem_turned, 1)

            def operands(kind, h, t):
                rows = slice(t * P, (t + 1) * P)
                band = slice(max(t - 1, 0) * P, (t + 1) * P)
                if kind == "X":
                    return qx[:, h // 2, rows], kx[:, h, :]
                if kind == "A0":
                    return qk[:, T_QA + h // 2, rows], qk[:, T_KA + h, band]
                if kind in ("A1", "A2"):
                    g = int(kind[1])
                    return qk[:, T_QA + 2 * g + h // 2, rows], qk[:, T_KA + 4 * g + h, rows]
                if kind == "B":
                    return qk[:, T_QB + h // 2, rows], qk[:, T_KB + 2 * (h // 4) + h % 2, band]
                return qk[:, T_QC + h // 2, rows], qk[:, T_KC + h, 0:(t + 1) * P]

            def key_gates(j):
                if j == 8:
                    pe.wait_ge(neg_ready, units_before[8])
                else:
                    pe.wait_ge(base_ready, TT * (j - 8))
                pe.matmul(ps[:, 3, :], ident[0:N_CH, j - 8:j - 7].to_broadcast([N_CH, P]), ncum_t[:, :], start=True,
                          stop=True).then_inc(ncum_ps, 1)

            def scores(j, banks=None):
                for b in banks or range(len(JOBS[j][0])):
                    units = JOBS[j][0][b]
                    bank = score_bank(j, b)
                    prev = [(jj, bb) for jj, bb in bank_list if jj < j and score_bank(jj, bb) == bank]
                    if prev:
                        pe.wait_ge(neg_ready, bank_units_end[prev[-1]])
                    for kind, h, t, c0, cols, at in units:
                        q, k = operands(kind, h, t)
                        ins = pe.matmul(ps[:, bank, c0:c0 + cols], q, k, start=True, stop=True)
                    ins.then_inc(score_ps, 1)

            def v_tile(kind, h, kb):
                if kind == "A0":
                    return va[:, kb, h * DH:(h + 1) * DH]
                if kind in ("A1", "A2"):
                    g = int(kind[1])
                    return va[:, kb, 256 * g + h * DH:256 * g + (h + 1) * DH]
                if kind == "B":
                    return vbc[:, kb, (h // 4) * DH:(h // 4 + 1) * DH]
                if kind == "C":
                    return vbc[:, kb, 128 + h * DH:128 + (h + 1) * DH]
                return vx[:, kb, h * DH:(h + 1) * DH]

            def turn_probs(n):
                j, g = group_list[n]
                offs = JOBS[j][1][g][0]
                pe.wait_ge(prob_pool if j in POOL_SCALES else prob_dve, scaled_for(j, g))
                if n >= 2:
                    pe.wait_ge(*pt_count(n - 2))
                buf = probx if j >= N_SELF else prob
                for c, at in enumerate(offs):
                    ins = pe.transpose(ps[:, 4 + n % 2, c * P:(c + 1) * P], buf[:, SLOT(j), at:at + P], ident[:, :])
                ins.then_inc(pt_ps, 1)

            def times_v(n):
                work = []
                for i in (n, n + 1):
                    j, g = group_list[i]
                    _, products, kind, h, first, last = JOBS[j][1][g]
                    m = acc_of[i]
                    pe.wait_ge(*pt_count(i))
                    if first and m >= 2:
                        if acc_kind[m - 2][0] == "X":
                            pe.wait_ge(oxl_done, m - 2 - (N_ACC - N_XACC) + 1)
                        else:
                            pe.wait_ge(acc_dve if acc_by_dve[m - 2] else acc_act, acc_count[m - 2])
                    src = ptx if j >= N_SELF else pt
                    work.append([(ps[acc_half(kind, h), 6 + m % 2, q0:q0 + cols], v_tile(kind, h, kb),
                                  src[:, i % PT_SLOTS, c0:c0 + cols], first and x == 0, last and x == len(products) - 1)
                                 for x, (kb, c0, cols, q0) in enumerate(products)])
                a, b = work
                for x in range(max(len(a), len(b))):
                    for one in (a, b):
                        y = x - max(len(a), len(b)) + len(one)
                        if y >= 0:
                            dst, lhs, rhs, start, stop = one[y]
                            ins = pe.matmul(dst, lhs, rhs, start=start, stop=stop, skip_group_check=True)
                            if y == len(one) - 1:
                                ins.then_inc(av_done, 1)

            for what, n in FRONT:
                if what == "scores":
                    if n == 0:
                        pe.wait_ge(proj_out, 18)
                        pe.wait_ge(zero_ready, 2)
                    scores(n)
                elif what == "piece":
                    p = n
                    if n == 18:
                        pe.wait_ge(proj_out, 6)
                    pe.wait_ge(lo_done, p + 1)
                    if p < PQB:
                        v_piece(p, 2 * (p - PVBC), 2, VBC_N, lambda t: (4 + t, 0, 0, 0), natural)
                    else:
                        m = p - PQB
                        pe.wait_ge(proj_out, 22 if m < 4 else 22 + m - 3)
                        tile_piece(p, 4 + (m + 3) % 4)
                elif what == "forward":
                    pe.wait_ge(neg_ready, units_before[4])
                    pe.wait_ge(parts_ready, 1)
                    pe.wait_ge(const_ready, 5)
                    pv = parts[:, :, :].rearrange("p c (t g x) -> p c t g x", t=TT, g=N_G)
                    for t in range(TT):
                        for g in range(2):
                            at = (t * 2 + g) * 24
                            for s in range(TT):
                                c = P * t - s + 3
                                ins = pe.matmul(ps[:, 0, at:at + 24], spread[:, c:c + P], pv[:, :, s, g + 1, :],
                                                start=(s == 0), stop=(s == TT - 1))
                    ins.then_inc(moved_ps, 1)
                    pe.wait_ge(lparts_ready, 1)
                    lv = lparts[:, :, :].rearrange("p c (t h) -> p c t h", t=TT)
                    for t in range(TT):
                        for s in range(t + 1):
                            m = upper[:, 0:P] if s == t else upper[:, P:2 * P]
                            ins = pe.matmul(ps[:, 1, 12 * t:12 * t + 12], m, lv[:, :, s, :], start=(s == 0), stop=(s == t))
                    ins.then_inc(cum_ps, 1)
                else:
                    pe.wait_ge(cum_ready, 1)
                    for t in range(TT):
                        ins = pe.transpose(ps[0:N_CH, 3, t * P:(t + 1) * P], cum[:, t, :], ident[:, :])
                    ins.then_inc(cumt_ps, 1)
                    pe.wait_ge(fparts_ready, 1)
                    fv = parts[:, :, 0:48].rearrange("p c (t g h) -> p c t g h", t=TT, g=N_G)
                    for g in range(2):
                        for s in range(TT):
                            at = (g * TT + s) * 12
                            for t in range(TT):
                                c = 384 + s - P * t
                                ins = pe.matmul(ps[:, 2, at:at + 12], shift[:, c:c + 4 * (P - 1) + 1:4], fv[:, :, t, g + 1, :],
                                                start=(t == 0), stop=(t == TT - 1))
                    ins.then_inc(back_ps, 1)
            pe.wait_ge(factor_ready, 2)
            pe.wait_ge(cumt_out, 1)
            pe.wait_ge(proj_out, 22 + 7)
            turn_probs(0)
            turn_probs(1)
            for i in range(N_GROUP_PAIRS):
                if i + 1 < N_GROUP_PAIRS:
                    turn_probs(2 * i + 2)
                    turn_probs(2 * i + 3)
                for what, j, b in SIDE[i]:
                    if what == "base":
                        key_gates(j)
                    else:
                        scores(j, [b])
                if i == 0:
                    pe.wait_ge(proj_out, 22 + 9)
                times_v(2 * i)

            def gate_iteration(i, first=False):
                for q in range(6):
                    p = PG + q
                    if first and q == 0:
                        pe.wait_ge(neg_ready, units_before[N_SELF])
                        pe.wait_ge(base_ready, TT * N_CH)
                    if first and q == 4:
                        pe.wait_ge(pt_act, N_GROUP_PAIRS)
                        pe.wait_ge(pt_dve, N_GROUP_PAIRS)
                    pe.wait_ge(lo_done, i * 8 + (p + 1))
                    if q == 0 and not first:
                        pe.wait_ge(merged_even, i)
                    if q == 1 and not first:
                        pe.wait_ge(merged_odd, i)
                    tile_piece(p, q)
                for b in range(2):
                    p = PG + 6 + b
                    pe.wait_ge(lo_done, i * 8 + (p + 1))
                    pe.wait_ge(o_ab_lo, N_OUT_AB)
                    pe.wait_ge(o_lo_done, KT - N_OUT_AB)
                    if first:
                        pe.wait_ge(acc_act, c_act - N_XACC)
                        pe.wait_ge(acc_dve, N_ACC_DVE)
                    pe.wait_ge(sig_done, i * 6 + (1 if b == 0 else 4))
                    wh, wl = (w[p % 2][:, :].rearrange("p (k c) -> p k c", k=KT) for w in (w_hi, w_lo))
                    for bank, (k0, k1) in zip((6, 7, 0) if b == 0 else (1, 2, 3), ((0, 2), (2, 6), (6, 8))):
                        for k in range(k0, k1):
                            ins = mm3(ps[:, bank, :], wh[:, k, :], wl[:, k, :], o_hi[:, k, :], o_lo[:, k, :], k == k0, k == k1 - 1)
                    ins.then_inc(piece_done, 1)

            gate_iteration(0, first=True)
            with pe.Fori(1, N_PAIR) as i:
                gate_iteration(i)

            def rows_part(p, k, t, n, a_hi, a_lo, start, stop):
                w_h, w_l = split_slot(p)
                cols = slice(n * 512, (n + 1) * 512)
                rows = slice(t * P, (t + 1) * P)
                return mm3(ps[:, 2 * t + n, :], a_hi[:, k, rows], a_lo[:, k, rows], w_h[:, cols], w_l[:, cols], start, stop)

            def rows_tail(p0, n_k, n_tail, t, a_hi, a_lo, ready=None):
                ks = range(n_k - n_tail, n_k)
                if t == 0:
                    for k in ks:
                        pe.wait_ge(lo_done, p0 + k + 1)
                        if ready:
                            ready(k)
                        for n in range(2):
                            ins = rows_part(p0 + k, k, t, n, a_hi, a_lo, k == 0, k == n_k - 1)
                            if k == n_k - 1:
                                ins.then_inc(rows_done, 1)
                    return
                for n in range(2):
                    for k in ks:
                        ins = rows_part(p0 + k, k, t, n, a_hi, a_lo, k == 0, k == n_k - 1)
                        if t == TT - 1 and n == 1:
                            ins.then_inc(piece_done, 1)
                    if t < TT - 1 or n == 0:
                        ins.then_inc(rows_done, 1)

            def turn_tile(k, t):
                pe.wait_ge(norm_done, TT * (k - 1) + t + 1)
                pe.wait_ge(y_done, 2 * (TT * (k - 1) + t + 1))
                for ins in turn(resid, t, 2 * t):
                    ins.then_inc(turned, 1)

            pe.wait_ge(merge_step, 12)
            for pair in ((2, 3), (0, 1)):
                if pair[0] == 2:
                    pe.wait_ge(sig_done, N_PAIR * 6)
                    pe.wait_ge(merged_even, N_PAIR)
                else:
                    pe.wait_ge(merged_odd, N_PAIR)
                for k in range(2):
                    pe.wait_ge(lo_done, PM + k + 1)
                    for t in pair:
                        for n in range(2):
                            ins = rows_part(PM + k, k, t, n, m_hi, m_lo, k == 0, False)
                    if pair[0] == 0:
                        ins.then_inc(piece_done, 1)
            rows_tail(PM, KT, N_TAIL, 0, m_hi, m_lo, lambda k: pe.wait_ge(merge_step, 6 * (k + 1)))
            rows_tail(PM, KT, N_TAIL, 1, m_hi, m_lo)
            turn_tile(1, 0)
            rows_tail(PM, KT, N_TAIL, 2, m_hi, m_lo)
            turn_tile(1, 1)
            rows_tail(PM, KT, N_TAIL, 3, m_hi, m_lo)
            turn_tile(1, 2)

            pe.wait_ge(mem_lo, 4)
            pe.wait_ge(turn_lo, 2 * TT + 2)
            for n in range(2):
                pe.wait_ge(lo_done, PKX + n + 1)
                tile_piece(PKX + n, n, memt_hi, memt_lo, slice(0, MEM))
            pe.wait_ge(turn_lo, 2 * TT + 4)
            for n in range(2):
                pe.wait_ge(lo_done, PVX + n + 1)
                v_piece_two(pe, PVX + n, w_hi, w_lo, memt_hi, memt_lo, ps, 4 * n, range(2), lambda t: (2, 256 * t), mm3, natural).then_inc(piece_done, 1)

            def queries(half_t):
                for n in range(2):
                    pe.wait_ge(lo_done, PXQ + n + 1)
                    ins = tile_piece(PXQ + n, 4 + 2 * half_t + n, cols=slice(256 * half_t, 256 * half_t + 256), signal=False)
                    ins.then_inc(xq_ps if half_t == 0 else piece_done, 1)

            pe.wait_ge(turn_lo, 2 * TT + 6)
            queries(0)
            turn_tile(1, 3)
            pe.wait_ge(xq_out, 2)
            pe.wait_ge(memkv_out, 3)
            pe.wait_ge(zero_ready, 5)
            scores(N_SELF)
            pe.wait_ge(turn_lo, 2 * TT + 8)
            queries(1)
            pe.wait_ge(xq_out, 4)
            scores(N_SELF + 1)
            gx, g_end = groups_before[N_SELF], groups_before[N_JOB]
            turn_probs(gx)
            turn_probs(gx + 1)
            for n in range(gx, g_end, 2):
                if n + 2 < g_end:
                    turn_probs(n + 2)
                    turn_probs(n + 3)
                times_v(n)
                if n == gx + 4:
                    pe.wait_ge(oxl_done, N_XH)
                    pe.wait_ge(neg_ready, units_before[N_JOB])
                    rows_tail(PXO, 2, 2, 0, ox_hi, ox_lo)
            rows_tail(PXO, 2, 2, 1, ox_hi, ox_lo)
            pe.wait_ge(oxl_done, 2 * N_XH)
            rows_tail(PXO, 2, 2, 2, ox_hi, ox_lo)
            turn_tile(2, 0)
            rows_tail(PXO, 2, 2, 3, ox_hi, ox_lo)
            turn_tile(2, 1)

            for half_t in range(2):
                pe.wait_ge(turn_lo, 4 * TT + 4 * (half_t + 1))
                for q in range(4):
                    pe.wait_ge(lo_done, PF + q + 1)
                    ins = tile_piece(PF + q, q, cols=slice(256 * half_t, 256 * half_t + 256), at=256 * half_t, signal=False)
                    if half_t == 1:
                        ins.then_inc(piece_done, 1)
                    elif q in (1, 2):
                        turn_tile(2, q + 1)

            def ffn_piece(i, q):
                p = PF + q
                pe.wait_ge(lo_done, i * 4 + (p + 1))
                wh, wl = (w[p % 2][:, :].rearrange("p (k c) -> p k c", k=KT) for w in (w_hi, w_lo))
                for k in range(KT):
                    ins = mm3(ps[:, q, :], wh[:, k, :], wl[:, k, :], xt_hi[:, k, :], xt_lo[:, k, :], k == 0, k == KT - 1)
                ins.then_inc(piece_done, 1)

            with pe.Fori(1, FF_PAIR) as i:
                for q in range(4):
                    if q == 0:
                        pe.wait_ge(silu_done, i * 2)
                    if q == 2:
                        pe.wait_ge(h_done, i * 2)
                    ffn_piece(i, q)

            for k in range(FF_T - N_TAIL):
                pe.wait_ge(lo_done, PO + k + 1)
                pe.wait_ge(h_done, k + 1)
                for t in MIX_ORDER:
                    if k == 0 and t < 2:
                        pe.wait_ge(h_done, FF_T - 1 + t)
                    for n in range(2):
                        ins = rows_part(PO + k, k, t, n, h_hi, h_lo, k == 0, False)
                ins.then_inc(piece_done, 1)
            for t in range(TT):
                rows_tail(PO, FF_T, N_TAIL, t, h_hi, h_lo, lambda k: pe.wait_ge(h_done, k + 1))


def v_piece_two(pe, p, w_hi, w_lo, x_hi, x_lo, ps, k0, tiles, place, mm3, pick):
    wh, wl = (w[p % 2][:, :].rearrange("p (k c) -> p k c", k=4) for w in (w_hi, w_lo))
    for kk in range(4):
        k = k0 + kk
        for t in tiles:
            bank, c0 = place(t)
            a_hi, a_lo = pick(x_hi, k, t), pick(x_lo, k, t)
            dst = ps[:, bank, c0:c0 + 256]
            first = k == 0 and c0 == 0
            pe.matmul(dst, a_hi, wh[:, kk, :], start=first, stop=False, skip_group_check=True)
            pe.matmul(dst, a_lo, wh[:, kk, :], start=False, stop=False, skip_group_check=True)
            ins = pe.matmul(dst, a_hi, wl[:, kk, :], start=False, stop=(k == KT - 1), skip_group_check=True)
    return ins


_INS = ["x", "mem", "w_in", "b_in", "attn_sinks", "w_branch_a", "w_branch_b", "w_branch_c", "w_mix_out", "ln1_g", "ln1_b",
        "w_xq", "w_xkv", "w_xo", "ln2_g", "ln2_b", "w_ffn_in", "w_ffn_out", "ln3_g", "ln3_b", "rel_bias"]


def kernel(**inputs):
    import concourse.bacc as _bacc
    from concourse.bass_utils import run_bass_kernel_spmd as _run

    nc = _bacc.Bacc("TRN2", target_bir_lowering=False, num_devices=1)
    arrays = {f"in_{name}": np.ascontiguousarray(inputs[name]) for name in _INS}
    arrays["in_one_hot"], arrays["in_seg_mask"] = table_constants()
    aps = {name[3:]: nc.dram_tensor(name, a.shape, mybir.dt.from_np(a.dtype), kind="ExternalInput").ap()
           for name, a in arrays.items()}
    out = nc.dram_tensor("out", (1, SEQ, D), F32, kind="ExternalOutput").ap()
    build_layer(nc, aps, out)
    r = _run(nc, [arrays], core_ids=[0])
    return r.results[0]["out"]
```
